# Optimizing a Trainium2 kernel written in Bass

```python
import math
import jax, jax.numpy as jnp
from jax import lax
import numpy as np

D_MODEL = 1024
BATCH = 1
SEQ = 2048
DEPTH = 1
DEC_BATCH = 1
DEC_SEQ = 32
PAST_LEN = 512

CHUNK = 64
MIX_WIDTH = D_MODEL
POOL_WIDTH = MIX_WIDTH // 2
POOL_WINDOWS = (2, 4, 8, 16)
POOL_GROUPS = len(POOL_WINDOWS)
POOL_GROUP_WIDTH = POOL_WIDTH // POOL_GROUPS
POOL_HIST = max(POOL_WINDOWS) - 1
SB_WIDTH = MIX_WIDTH - POOL_WIDTH
SB_HEAD_DIM = 64
SB_HEADS = SB_WIDTH // SB_HEAD_DIM
SB_SCALE = 1.0 / math.sqrt(SB_HEAD_DIM)
QBLOCK = 128
D_FF = int(math.ceil(8 * D_MODEL / 3 / 256)) * 256
DEEPNORM_ALPHA = (2 * DEPTH) ** 0.25
DEEPNORM_BETA = (8 * DEPTH) ** -0.25
LN_EPS = 1e-5

kernel_name = "pool_stickbreak_hybrid_stream_step"

def layer_norm(x, gain=None, bias=None):
    xf = x.astype(jnp.float32)
    mu = jnp.mean(xf, axis=-1, keepdims=True)
    xc = xf - mu
    var = jnp.mean(xc * xc, axis=-1, keepdims=True)
    y = xc * lax.rsqrt(var + LN_EPS)
    if gain is not None:
        y = y * gain.astype(jnp.float32) + bias.astype(jnp.float32)
    return y

def multiscale_pool(u_ext, n_hist, w_pool_l, scale_l):
    b, l, c = u_ext.shape
    t = l - n_hist
    uf = u_ext.astype(jnp.float32)
    cs = jnp.concatenate([jnp.zeros((b, 1, c), jnp.float32), jnp.cumsum(uf, axis=1)], axis=1)
    end = n_hist + 1 + jnp.arange(t)
    cs_end = cs[:, n_hist + 1:]
    cur = uf[:, n_hist:]
    groups = []
    for g, w in enumerate(POOL_WINDOWS):
        sl = slice(g * POOL_GROUP_WIDTH, (g + 1) * POOL_GROUP_WIDTH)
        start = jnp.maximum(end - w, 0)
        count = (end - start).astype(jnp.float32)[None, :, None]
        win_sum = cs_end[..., sl] - jnp.take(cs[..., sl], start, axis=1)
        groups.append(win_sum / count - cur[..., sl])
    pooled = jnp.stack(groups, axis=2)
    mixed = jnp.einsum("btgc,gcd->btgd", pooled, w_pool_l.astype(jnp.float32)).reshape(b, t, c)
    return mixed * scale_l.astype(jnp.float32)

def stick_breaking_block(q_blk, q_pos, k, v, k_pos):
    z = jnp.einsum("bqhd,bkhd->bhqk", q_blk.astype(jnp.float32), k.astype(jnp.float32)) * SB_SCALE
    mask = k_pos[None, :] < q_pos[:, None]
    log_1mb = jnp.where(mask, jax.nn.log_sigmoid(-z), 0.0)
    log_a = jax.nn.log_sigmoid(z) + lax.cumsum(log_1mb, axis=3, reverse=True) - log_1mb
    a = jnp.where(mask, jnp.exp(log_a), 0.0)
    return jnp.einsum("bhqk,bkhd->bqhd", a, v.astype(jnp.float32))

def stick_breaking_prompt(q, k, v):
    b, s, h, d = q.shape
    nb = s // QBLOCK
    qb = q.reshape(b, nb, QBLOCK, h, d).transpose(1, 0, 2, 3, 4)
    k_pos = jnp.arange(s)

    def one_block(args):
        blk, i = args
        q_pos = i * QBLOCK + jnp.arange(QBLOCK)
        return stick_breaking_block(blk, q_pos, k, v, k_pos)

    out = lax.map(one_block, (qb, jnp.arange(nb)))
    return out.transpose(1, 0, 2, 3, 4).reshape(b, s, h, d)

def stick_breaking_sample(q, k_all, v_all, n_past):
    t = q.shape[1]
    k_pos = jnp.arange(k_all.shape[1])
    q_pos = n_past + jnp.arange(t)
    return stick_breaking_block(q, q_pos, k_all, v_all, k_pos)

def token_mixers(h, w_in_l, w_pool_l, pool_scale_l, hist):
    b, t, _ = h.shape
    proj = h @ w_in_l
    u = proj[..., :POOL_WIDTH]
    o = POOL_WIDTH
    q = proj[..., o:o + SB_WIDTH].reshape(b, t, SB_HEADS, SB_HEAD_DIM)
    k = proj[..., o + SB_WIDTH:o + 2 * SB_WIDTH].reshape(b, t, SB_HEADS, SB_HEAD_DIM)
    v = proj[..., o + 2 * SB_WIDTH:o + 3 * SB_WIDTH].reshape(b, t, SB_HEADS, SB_HEAD_DIM)
    if hist is None:
        u_ext, n_hist = u, 0
        sb = stick_breaking_prompt(q, k, v)
    else:
        cache_k_l, cache_v_l, pool_l = hist
        u_ext, n_hist = jnp.concatenate([pool_l, u], axis=1), POOL_HIST
        sb = stick_breaking_sample(q, jnp.concatenate([cache_k_l, k], axis=1),
                                   jnp.concatenate([cache_v_l, v], axis=1), cache_k_l.shape[1])
    pool_out = multiscale_pool(u_ext, n_hist, w_pool_l, pool_scale_l)
    mixed = jnp.concatenate([pool_out, sb.reshape(b, t, SB_WIDTH)], axis=-1).astype(h.dtype)
    return mixed, k, v, u_ext[:, -POOL_HIST:]

def run_trunk(x, c, hist, w_ada, b_ada, w_in, w_pool, pool_scale, w_o,
              ln1_g, ln1_b, w_gu, w_down, ln2_g, ln2_b):
    dt = x.dtype
    ks, vs, ps = [], [], []
    cond = jax.nn.silu(c)
    for l in range(DEPTH):
        mod = (cond @ w_ada[l] + b_ada[l]).astype(jnp.float32)[:, None, :]
        sh1, sc1, g1, sh2, sc2, g2 = jnp.split(mod, 6, axis=-1)
        h = (layer_norm(x) * (1.0 + sc1) + sh1).astype(dt)
        layer_hist = None if hist is None else (hist[0][l], hist[1][l], hist[2][l])
        mixed, k, v, pool_state = token_mixers(h, w_in[l], w_pool[l], pool_scale[l], layer_hist)
        mix_out = (mixed @ w_o[l]).astype(jnp.float32)
        x = layer_norm(DEEPNORM_ALPHA * x.astype(jnp.float32) + g1 * mix_out, ln1_g[l], ln1_b[l]).astype(dt)
        h = (layer_norm(x) * (1.0 + sc2) + sh2).astype(dt)
        gu = h @ w_gu[l]
        ff = ((jax.nn.silu(gu[..., :D_FF]) * gu[..., D_FF:]) @ w_down[l]).astype(jnp.float32)
        x = layer_norm(DEEPNORM_ALPHA * x.astype(jnp.float32) + g2 * ff, ln2_g[l], ln2_b[l]).astype(dt)
        ks.append(k)
        vs.append(v)
        ps.append(pool_state)
    return x, jnp.stack(ks), jnp.stack(vs), jnp.stack(ps)

def setup_inputs(seed: int = 0) -> dict:
    key = jax.random.key(seed)
    kk = jax.random.split(key, 20)
    f32 = jnp.float32
    nrm = lambda k, shape: jax.random.normal(k, shape, f32)
    v_col = jnp.concatenate([jnp.ones((POOL_WIDTH + 2 * SB_WIDTH,), f32),
                             jnp.full((SB_WIDTH,), DEEPNORM_BETA, f32)])
    return {
        "x_prompt": nrm(kk[0], (BATCH, SEQ, D_MODEL)),
        "x_sample": nrm(kk[1], (DEC_BATCH, DEC_SEQ, D_MODEL)),
        "cache_k": nrm(kk[2], (DEPTH, DEC_BATCH, PAST_LEN, SB_HEADS, SB_HEAD_DIM)),
        "cache_v": DEEPNORM_BETA * nrm(kk[3], (DEPTH, DEC_BATCH, PAST_LEN, SB_HEADS, SB_HEAD_DIM)),
        "state_pool": nrm(kk[4], (DEPTH, DEC_BATCH, POOL_HIST, POOL_WIDTH)),
        "c_prompt": nrm(kk[5], (BATCH, D_MODEL)),
        "c_sample": nrm(kk[6], (DEC_BATCH, D_MODEL)),
        "w_ada": 0.5 * D_MODEL ** -0.5 * nrm(kk[7], (DEPTH, D_MODEL, 6 * D_MODEL)),
        "b_ada": 0.02 * nrm(kk[8], (DEPTH, 6 * D_MODEL)),
        "w_in": D_MODEL ** -0.5 * nrm(kk[9], (DEPTH, D_MODEL, POOL_WIDTH + 3 * SB_WIDTH)) * v_col,
        "w_pool": POOL_GROUP_WIDTH ** -0.5 * nrm(kk[10], (DEPTH, POOL_GROUPS, POOL_GROUP_WIDTH, POOL_GROUP_WIDTH)),
        "pool_scale": 1.0 + 0.1 * nrm(kk[11], (DEPTH, POOL_WIDTH)),
        "w_o": DEEPNORM_BETA * MIX_WIDTH ** -0.5 * nrm(kk[12], (DEPTH, MIX_WIDTH, D_MODEL)),
        "ln1_g": 1.0 + 0.02 * nrm(kk[13], (DEPTH, D_MODEL)),
        "ln1_b": 0.02 * nrm(kk[14], (DEPTH, D_MODEL)),
        "w_gu": D_MODEL ** -0.5 * nrm(kk[15], (DEPTH, D_MODEL, 2 * D_FF)),
        "w_down": DEEPNORM_BETA * D_FF ** -0.5 * nrm(kk[16], (DEPTH, D_FF, D_MODEL)),
        "ln2_g": 1.0 + 0.02 * nrm(kk[17], (DEPTH, D_MODEL)),
        "ln2_b": 0.02 * nrm(kk[18], (DEPTH, D_MODEL)),
    }

def reference(x_prompt, x_sample, cache_k, cache_v, state_pool, c_prompt, c_sample,
              w_ada, b_ada, w_in, w_pool, pool_scale, w_o, ln1_g, ln1_b,
              w_gu, w_down, ln2_g, ln2_b):
    y_prompt, new_k_prompt, new_v_prompt, new_pool_prompt = run_trunk(
        x_prompt, c_prompt, None, w_ada, b_ada, w_in, w_pool, pool_scale, w_o,
        ln1_g, ln1_b, w_gu, w_down, ln2_g, ln2_b)
    y_sample, new_k_sample, new_v_sample, new_pool_sample = run_trunk(
        x_sample, c_sample, (cache_k, cache_v, state_pool), w_ada, b_ada, w_in, w_pool, pool_scale, w_o,
        ln1_g, ln1_b, w_gu, w_down, ln2_g, ln2_b)
    return (y_prompt, y_sample, new_k_prompt, new_v_prompt, new_pool_prompt,
            new_k_sample, new_v_sample, new_pool_sample)


_drawn_inputs = setup_inputs


def setup_inputs(seed=0):
    import zlib

    import numpy as np

    out = dict(_drawn_inputs(seed))
    spreads = {}
    factors = {'cache_k': 8.0,
     'cache_v': 7.297,
     'state_pool': 4.718,
     'pool_scale': 5.304,
     'ln1_g': 20.531,
     'ln1_b': 21.55,
     'ln2_g': 23.292,
     'ln2_b': 23.719,
     'w_gu': 3.612,
     'w_down': 3.615}
    for name, (base, spread) in spreads.items():
        noise = np.random.default_rng([zlib.crc32(name.encode()), seed]).standard_normal(out[name].shape)
        drawn = base * np.exp(spread * noise) if base else spread * noise
        out[name] = __import__('jax').numpy.asarray(drawn.astype(out[name].dtype))
    for name, factor in factors.items():
        out[name] = (out[name] * factor).astype(out[name].dtype)
    return out
```

```python
import concourse.bass as bass
from concourse import mybir
from contextlib import ExitStack

f32 = mybir.dt.float32
f16 = mybir.dt.float16
bf16 = mybir.dt.bfloat16
i32 = mybir.dt.int32
ALU = mybir.AluOpType
ACT = mybir.ActivationFunctionType
AX = mybir.AxisListType
RMAX = bass.bass_isa.ReduceOp.max

P = 128
D = 1024
KD = D // P
SEQ = 2048
NT = SEQ // P
TS = 32
TOK = SEQ + TS
PAST = 512
HIST = 15
PW = 512
SBW = 512
HD = 64
NH = SBW // HD
NPAIR = NH // 2
FF = 2816
NF = FF // P
BLK = 512
ALPHA = 2.0 ** 0.25
EPS = 1e-5
SCALE = HD ** -0.5
TOP = 14
FAR = -1.0e30
HW = P * KD * 2
SBCOLS = 1056
LN_ROOT = 32.0


def encoder_step(nc, x_prompt, x_sample, cache_k, cache_v, state_pool, c_prompt, c_sample,
                 w_ada, b_ada, w_in, w_pool, pool_scale, w_o, ln1_g, ln1_b,
                 w_gu, w_down, ln2_g, ln2_b,
                 y_prompt, y_sample, new_k_prompt, new_v_prompt, new_pool_prompt,
                 new_k_sample, new_v_sample, new_pool_sample):
    ctx = ExitStack()
    with ctx:
        def sb(name, shape, dt):
            return ctx.enter_context(nc.sbuf_tensor(name, shape, dt))

        def sem(name):
            return ctx.enter_context(nc.semaphore(name))

        q_t_dram = nc.dram_tensor("q_t_dram", (NPAIR, P, TOK), f32).ap()
        k_t_dram = nc.dram_tensor("k_t_dram", (NPAIR, P, TOK), f32).ap()
        pool_dram = nc.dram_tensor("pool_dram", (4, P, TOK), f32).ap()
        x1_dram = nc.dram_tensor("x1_dram", (TOK, D), f32).ap()

        ident = sb("ident", [P, P], f32)
        ident_b = sb("ident_b", [P, P], bf16)
        mask_b = sb("mask_b", [P, P], bf16)
        ln2_rows = sb("ln2_rows", [P, 2, D], f32)
        mod_t = sb("mod_t", [P, 5, KD, 2], f32)
        col = sb("col", [P, 64], f32)
        small = sb("small", [P, 96], f32)
        hidden_t = sb("hidden_t", [P, NT + 1, KD, 2, P], f16)
        WORK = 33000
        work = sb("work", [P, WORK], f32)
        ps = ctx.enter_context(nc.psum_tensor("ps", [P, 8, 512], f32))

        def w32(at, n):
            assert at + n <= WORK, (at, n)
            return work[:, at:at + n]

        def w16(at, n):
            assert at + n // 2 <= WORK, (at, n)
            return work[:, at:at + n // 2].bitcast(f16)

        C_NEGHALF, C_SH, C_FH, C_SH2, C_FH2 = 0, 1, 2, 3, 4
        C_SGU, C_SWD, C_SWO, C_SMIX = 5, 6, 7, 8
        C_FGU, C_FWD, C_FWO, C_FMIX, C_SHID, C_FHID = 9, 10, 11, 12, 13, 14
        C_F1, C_F2, C_FWOMIX, C_FDOWN = 15, 16, 17, 18
        C_W = 20
        C_EPS = 19
        C_PSCALE = 24
        C_BOUND = 28
        C_POOLMAX = 36
        C_VMAX = 40
        C_INV = 46

        def c1(i, n=1):
            return col[:, i:i + n]

        A_X = [w32(0, 1024), w32(1024, 1024)]
        A_XH = [w32(2048, 1024), w32(3072, 1024)]
        A_HF = [w32(4096, 1024), w32(5120, 1024)]
        A_WADA = w32(6144, 8192).rearrange("p (s k n) -> p s k n", s=2, k=KD)
        A_BROW = w32(14336, 6144)
        A_MROW = w32(20480, 6144)
        A_CROW = w32(26624, 128)
        A_CT = w32(26752, 16)
        A_CSIG = w32(26768, 16)
        A_HISTROW = w32(26784, 512)
        A_STAT = [w32(27296, 16), w32(27312, 16)]
        A_RS = [w32(27328, 4), w32(27332, 4)]
        B_RAW = [w32(6144, 1024), w32(7168, 1024)]
        B_HL = [w16(8192, 2048), w16(9216, 2048)]
        UW = 2112
        B_U = w32(10240, UW)
        B_S = [w32(12352, UW), w32(14464, UW)]
        B_VT = [w32(12352, TOK), w32(14464, TOK)]
        B_STG = [w32(16576, 512), w32(17088, 512)]
        B_WPOOL = w32(17600, 512)
        B_NPOOL = w32(18112, 1024)
        B_BIG = w32(19200, 9472)
        B_CV = w32(28700, 2048)
        HIST_T = w32(30748, 60)
        C_Q = w32(0, 2048)
        C_K = w32(2048, 2048)
        C_V = w32(4096, 2048).rearrange("p (i c) -> p i c", c=P)
        PB = 516
        C_PR = w32(6144, 8 * PB)
        C_A = w32(10272, 4096).rearrange("p (s j n) -> p s j n", s=2, j=4)
        C_AT = [w32(14368 + 512 * i, 512) for i in range(4)]
        C_ST = [w32(16416, 512), w32(16928, 512)]
        C_POOL = w32(17440, TOK)
        C_CK = w32(19520, 2048).rearrange("p (i c) -> p i c", c=512)
        C_CKT = w32(21568, 2048).rearrange("p (h t) -> p h t", h=4)
        C_QS = w32(23616, 128).rearrange("p (h t) -> p h t", h=4)
        C_KS = w32(23744, 128).rearrange("p (h t) -> p h t", h=4)
        C_VN = w32(23872, 512)
        C_SP = [w32(24384, 548), w32(24932, 548)]
        C_SA = [w32(25480, 544), w32(26024, 544)]
        C_SAT = [w32(26568, 640), w32(27208, 640)]
        C_SST = w32(27848, 128)
        D_WO = w16(0, 16384).rearrange("p (h k n) -> p h k n", h=2, k=KD)
        D_RAW = [w32(8192, 1024), w32(9216, 1024)]
        D_X = [w32(10240, 1024), w32(11264, 1024)]
        D_R = [w32(12288, 1024), w32(13312, 1024)]
        D_X1 = [w32(14336, 1024), w32(15360, 1024)]
        D_XH = [w32(16384, 1024), w32(17408, 1024)]
        D_HF = [w32(18432, 1024), w32(19456, 1024)]
        D_G1 = w32(20480, 2048).rearrange("p (b n) -> p b n", b=2)
        D_LN1 = w32(22528, 2048).rearrange("p (b n) -> p b n", b=2)
        D_STAT = [w32(27296, 16), w32(27312, 16)]
        D_G1ROW = w32(30810, 1024)
        E_HID = w16(0, NF * 2 * SBCOLS).rearrange("p (j h t) -> p j h t", j=NF, h=2)
        E0 = NF * SBCOLS
        E_GRAW = w32(E0, 2048).rearrange("p (k w n) -> p k w n", k=KD, w=2)
        E_GHL = [w16(E0 + 2048 + 2048 * s, 4096).rearrange("p (h k w n) -> p h k w n", h=2, k=KD, w=2)
                 for s in range(2)]
        E_DRAW = w32(E0, 1408).rearrange("p (j n) -> p j n", n=P)
        E_DHL = [w16(E0 + 1408 + 2816 * s, 5632).rearrange("p (h j n) -> p h j n", h=2, j=NF)
                 for s in range(2)]
        E1 = E0 + 1408 + 5632
        E_SIG = w32(E1, 512)
        E_T = w32(E1 + 512, 512)
        E_H = w32(E1 + 1024, 512)
        E_X1 = w32(E1 + 1536, 1024)
        E_STAT = w32(32980, 16)
        B_SEL = w32(32600, 256).rearrange("p (b m) -> p b m", b=2)

        consts_set = sem("consts_set")
        crow_in, brow_in, hist_in = sem("crow_in"), sem("brow_in"), sem("hist_in")
        wada_in = [sem("wada_in0"), sem("wada_in1")]
        x_in = [sem("x_in0"), sem("x_in1")]
        misc_in = sem("misc_in")
        ct_mm, csig_set, ct_set = sem("ct_mm"), sem("csig_set"), sem("ct_set")
        ada_mm, ada_row = sem("ada_mm"), sem("ada_row")
        modt_mm, mod_max, mod_ar, mod_set = sem("modt_mm"), sem("mod_max"), sem("mod_ar"), sem("mod_set")
        dve = sem("dve_steps")
        pool_steps = sem("pool_steps")
        a_aggr, a_rstd, a_xhat = sem("a_aggr"), sem("a_rstd"), sem("a_xhat")
        a_tr, a_full, a_hi, a_lo = sem("a_tr"), sem("a_full"), sem("a_hi"), sem("a_lo")
        hist_mm, hist_set = sem("hist_mm"), sem("hist_set")
        w_in_raw = [sem("w_in_raw0"), sem("w_in_raw1")]
        w_mx, w_ar, w_s, w_hi, w_lo = sem("w_mx"), sem("w_ar"), sem("w_s"), sem("w_hi"), sem("w_lo")
        proj_mm, proj_out = sem("proj_mm"), sem("proj_out")
        pooled_set, wpool_mm, wpool_out, rmax_set = sem("pooled_set"), sem("wpool_mm"), sem("wpool_out"), sem("rmax_set")
        pool_stored = sem("pool_stored")
        npool_mm, npool_out = sem("npool_mm"), sem("npool_out")
        q_stored = [sem("q_stored0"), sem("q_stored1")]
        k_stored = [sem("k_stored0"), sem("k_stored1")]
        kvt_mm, kvt_out = sem("kvt_mm"), sem("kvt_out")
        kv_stored = [sem("kv_stored0"), sem("kv_stored1")]
        big_in, big_mx, vmax_set = sem("big_in"), sem("big_mx"), sem("vmax_set")
        cv_in = sem("cv_in")
        fin_max, fin_ar, fin_set = sem("fin_max"), sem("fin_ar"), sem("fin_set")
        out_small = sem("out_small")
        head_in = [sem("head_in0"), sem("head_in1")]
        pool_back = sem("pool_back")
        pool_split = sem("pool_split")
        z_mm, sg_set, be_set, scan_set, prod_set = (sem("z_mm"), sem("sg_set"), sem("be_set"),
                                                    sem("scan_set"), sem("prod_set"))
        at_mm, at_act, at_dve, av_mm = sem("at_mm"), sem("at_act"), sem("at_dve"), sem("av_mm")
        o_scaled, o_split = sem("o_scaled"), sem("o_split")
        smp_in = sem("smp_in")
        ck_mm, ck_set, sz_mm, ssig, sprod, sat_mm, sat_set, so_mm, so_split = (
            sem("ck_mm"), sem("ck_set"), sem("sz_mm"), sem("ssig"), sem("sprod"), sem("sat_mm"),
            sem("sat_set"), sem("so_mm"), sem("so_split"))
        g1_mm, g1_set = sem("g1_mm"), sem("g1_set")
        wo_raw = [sem("wo_raw0"), sem("wo_raw1")]
        wo_hi, wo_lo = sem("wo_hi"), sem("wo_lo")
        dx_in = [sem("dx_in0"), sem("dx_in1")]
        ln1_in = sem("ln1_in")
        d_mm, d_mo, d_res, d_aggr1, d_rstd1 = sem("d_mm"), sem("d_mo"), sem("d_res"), sem("d_aggr1"), sem("d_rstd1")
        d_x1, d_aggr2, d_rstd2, d_xhat = sem("d_x1"), sem("d_aggr2"), sem("d_rstd2"), sem("d_xhat")
        x1_stored = [sem("x1_stored0"), sem("x1_stored1")]
        d_tr, d_full, d_hi, d_lo = sem("d_tr"), sem("d_full"), sem("d_hi"), sem("d_lo")
        gu_raw, gu_hi, gu_lo = sem("gu_raw"), sem("gu_hi"), sem("gu_lo")
        gu_mm, sig_set, hid_set, hid_hi, hid_lo = sem("gu_mm"), sem("sig_set"), sem("hid_set"), sem("hid_hi"), sem("hid_lo")
        wd_raw, wd_hi, wd_lo = sem("wd_raw"), sem("wd_hi"), sem("wd_lo")
        dn_mm, dn_out = sem("dn_mm"), sem("dn_out")
        e_x1, e_tr, e_res, e_aggr, e_rstd, e_y, y_stored = (sem("e_x1"), sem("e_tr"), sem("e_res"),
                                                  sem("e_aggr"), sem("e_rstd"), sem("e_y"), sem("y_stored"))

        class Steps:

            def __init__(self, eng, sem_):
                self.eng, self.sem, self.n, self.reg, self.lo, self.per = eng, sem_, 0, None, 0, 0

            def done(self, ins):
                ins.then_inc(self.sem, 1)
                self.n += 1

            def wait(self):
                if self.reg is None:
                    self.eng.wait_ge(self.sem, self.n)
                else:
                    self.eng.wait_ge(self.sem, (self.reg - self.lo) * self.per + self.n)

            def enter(self, reg, lo, per):
                self.reg, self.lo, self.per, self.entry = reg, lo, per, self.n

            def leave(self, count):
                assert self.n - self.entry == self.per, (self.n - self.entry, self.per)
                self.n = self.entry + self.per * count
                self.reg = None

        BLKS = [(0, BLK), (1, BLK), (2, BLK), (3, BLK), (4, TS)]

        def moving(k, hl, blk):
            if blk < 4:
                return hidden_t[:, 4 * blk:4 * blk + 4, k, hl, :]
            return hidden_t[:, NT, k, hl, 0:TS]

        def bank(b, n, blk):
            return ps[:, b, 0:n].rearrange("p (a t) -> p a t", t=P) if blk < 4 else ps[:, b, 0:n]

        TERMS = [(0, 0), (0, 1), (1, 0)]
        PRW = C_PR.rearrange("p (j s n) -> p j s n", j=4, s=2)
        UNITS = [(b, kc) for b in range(4) for kc in range(b, -1, -1)]
        NU = len(UNITS)
        xp_t = x_prompt.rearrange("b (i p) d -> (b i) p d", p=P)
        x1_t = x1_dram[0:SEQ, :].rearrange("(i p) d -> i p d", p=P)
        yp_t = y_prompt.rearrange("b (i p) d -> (b i) p d", p=P)
        w_in_c = w_in[0].rearrange("(k p) (c n) -> c p k n", p=P, n=P)
        w_gu_c = w_gu[0].rearrange("(k p) (w j n) -> j w p k n", p=P, w=2, n=P)
        w_dn_c = w_down[0].rearrange("(j p) (c n) -> c p j n", p=P, n=P)
        nk_p = new_k_prompt[0, 0].rearrange("(i p) h d -> i p (h d)", p=P)
        nv_p = new_v_prompt[0, 0].rearrange("(i p) h d -> i p (h d)", p=P)
        nk_s = new_k_sample[0, 0].rearrange("t h d -> t (h d)")
        nv_s = new_v_sample[0, 0].rearrange("t h d -> t (h d)")
        BIGS = [(w_gu, 0, 5632), (w_down, 5632, 2816), (w_o, 8448, 1024)]
        bigs_flat = [w[0].rearrange("a b -> (a b)").rearrange("(p n) -> p n", p=P) for w, _, _ in BIGS]

        block = ctx.enter_context(nc.Block())

        @block.sync
        def _(sp):
            sp.dma_start(A_CROW[0:KD, :], c_prompt.rearrange("b (k p) -> (b k) p", p=P)).then_inc(crow_in, 16)
            sp.dma_start(A_CROW[KD:2 * KD, :], c_sample.rearrange("b (k p) -> (b k) p", p=P)).then_inc(crow_in, 16)
            for b in range(2):
                sp.dma_start(A_BROW[b:b + 1, :], b_ada[0:1, :]).then_inc(brow_in, 16)
            w_ada_c = w_ada[0].rearrange("(k p) (j n) -> j p k n", p=P, n=512)

            def load_ada(j, s):
                sp.dma_start(A_WADA[:, s, :, :], w_ada_c[j]).then_inc(wada_in[s], 16)

            def load_x(t, s):
                sp.dma_start(A_X[s], xp_t[t]).then_inc(x_in[s], 16)

            load_ada(0, 0)
            load_ada(1, 1)
            load_x(0, 0)
            load_x(1, 1)
            for s in range(2):
                sp.wait_ge(ada_mm, s + 1)
                load_ada(2 + s, s)
            sp.dma_start(A_HISTROW[0:HIST, :], state_pool[0, 0]).then_inc(hist_in, 16)
            sp.dma_start(ln2_rows[:, 0, :], ln2_g[0:1, :].partition_broadcast(P)).then_inc(misc_in, 16)
            sp.dma_start(ln2_rows[:, 1, :], ln2_b[0:1, :].partition_broadcast(P)).then_inc(misc_in, 16)
            sp.dma_start(col[:, C_PSCALE:C_PSCALE + 4],
                         pool_scale[0].rearrange("(g p) -> p g", p=P),
                         allow_slow_non_contiguous=True).then_inc(misc_in, 16)
            sp.dma_start(B_CV.rearrange("p (i c) -> p i c", c=512),
                         cache_v[0, 0].rearrange("(i p) h d -> p i (h d)", p=P)).then_inc(cv_in, 16)

            def step_a(q, u):
                sp.wait_ge(ada_mm, 2 * q + u + 3)
                load_ada(2 * q + u + 4, u)
                for s in range(2):
                    sp.wait_ge(a_xhat, 4 * q + 2 * u + s + 1)
                    load_x(4 * q + 2 * u + 2 + s, s)

            with sp.Fori(0, 3) as q:
                for u in range(2):
                    step_a(q, u)
            step_a(3, 0)
            sp.wait_ge(ada_mm, 10)
            load_ada(11, 1)
            sp.wait_ge(a_xhat, 15)
            sp.dma_start(A_X[0][0:TS, :], x_sample[0]).then_inc(x_in[0], 16)

            def load_w(c, s):
                sp.dma_start(B_RAW[s].rearrange("p (k n) -> p k n", k=KD), w_in_c[c]).then_inc(w_in_raw[s], 16)

            sp.wait_ge(ada_mm, 12)
            sp.wait_ge(ada_row, 12)
            sp.dma_start(B_WPOOL.rearrange("p (g n) -> p g n", g=4),
                         w_pool[0].rearrange("g p n -> p g n")).then_inc(misc_in, 16)
            load_w(0, 0)
            load_w(1, 1)

            def next_w(c, s):
                sp.wait_ge(w_lo, c + 1)
                load_w(c + 2, s)

            def store_pool(g):
                sp.wait_ge(wpool_out, 5 * (g + 1))
                sp.dma_start(pool_dram[g], B_S[g % 2][:, 0:TOK]).then_inc(pool_stored, 16)

            for g in range(4):
                next_w(g, g % 2)
                if g:
                    store_pool(g - 1)

            with sp.Fori(0, 2) as i:
                for u in range(2):
                    next_w(4 + 2 * i + u, u)
                    sp.wait_ge(proj_out, 5 * (2 * i + u) + 25)
                    sp.dma_start(q_t_dram[2 * i + u], B_BIG[:, TOK * u:TOK * (u + 1)]).then_inc(q_stored[u], 16)
            store_pool(3)
            for s in range(2):
                sp.wait_ge(q_stored[s], 32)

            def load_big(c):
                for (w, at, n), flat in zip(BIGS, bigs_flat):
                    sp.dma_start(B_BIG[:, at:at + n], flat[:, bass.ds(c * n, n)]).then_inc(big_in, 16)

            def store_rows(c, u, prompt, sample):
                for g in range(5):
                    sp.wait_ge(kvt_out, 5 * c + g + 1)
                    slot = (u + g) % 2
                    ch = (c % 4 if isinstance(c, int) else c)
                    if g < 4:
                        dst = prompt[4 * g:4 * g + 4, :, bass.ds(ch * P, P)].rearrange("i p c -> p i c")
                        sp.dma_start(dst, B_STG[slot].rearrange("p (i c) -> p i c", c=P)).then_inc(kv_stored[slot], 16)
                    else:
                        sp.dma_start(sample[:, bass.ds(ch * P, P)], B_STG[slot][0:TS, 0:P]).then_inc(kv_stored[slot], 16)

            load_big(0)
            with sp.Fori(0, 2) as i:
                for u in range(2):
                    c = 2 * i + u
                    next_w(8 + c, u)
                    sp.wait_ge(proj_out, 5 * c + 45)
                    sp.dma_start(k_t_dram[c], B_VT[u]).then_inc(k_stored[u], 16)
                    store_rows(c, u, nk_p, nk_s)
                    sp.wait_ge(big_mx, c + 1)
                    load_big(c + 1)
            for c in range(4, 8):
                if c < 6:
                    next_w(8 + c, c % 2)
                store_rows(c, c % 2, nv_p, nv_s)
                if c < 7:
                    sp.wait_ge(big_mx, c + 1)
                    load_big(c + 1)
            sp.wait_ge(npool_out, 4)
            sp.dma_start(new_pool_prompt[0, 0], B_NPOOL[0:HIST, 0:PW]).then_inc(out_small, 16)
            sp.dma_start(new_pool_sample[0, 0], B_NPOOL[0:HIST, PW:2 * PW]).then_inc(out_small, 16)
            for s in range(2):
                sp.wait_ge(k_stored[s], 32)
                sp.wait_ge(kv_stored[s], 320)
            sp.wait_ge(fin_set, 1)
            sp.wait_ge(out_small, 32)

            def load_pool(g):
                sp.dma_start(C_POOL, pool_dram[g]).then_inc(pool_back, 16)

            def load_head(hp, e):
                r = slice(HD * e, HD * e + HD)
                sp.dma_start(C_Q[r, :], q_t_dram[hp, r, 0:SEQ]).then_inc(head_in[e], 16)
                sp.dma_start(C_K[r, :], k_t_dram[hp, r, 0:SEQ]).then_inc(head_in[e], 16)
                sp.dma_start(C_V[:, :, r], nv_p[:, :, bass.ds(hp * P + HD * e, HD)].rearrange("i p c -> p i c")
                             ).then_inc(head_in[e], 16)

            sp.wait_ge(pool_stored, 64)
            load_head(0, 0)
            load_head(0, 1)
            load_pool(0)
            for g in range(1, 4):
                sp.wait_ge(pool_split, g)
                load_pool(g)
            sp.dma_start(C_CK, cache_k[0, 0].rearrange("(i p) h d -> p i (h d)", p=P)).then_inc(smp_in, 16)
            sp.dma_start(C_QS, q_t_dram[:, :, SEQ:TOK].rearrange("h p t -> p h t")).then_inc(smp_in, 16)
            sp.dma_start(C_KS, k_t_dram[:, :, SEQ:TOK].rearrange("h p t -> p h t")).then_inc(smp_in, 16)
            sp.dma_start(C_VN[0:TS, :], nv_s).then_inc(smp_in, 16)
            with sp.Fori(1, NPAIR) as hp:
                for e in range(2):
                    sp.wait_ge(av_mm, (hp - 1) * 8 * NU + 4 * NU * (e + 1))
                    load_head(hp, e)

            sp.wait_ge(so_split, 1)
            w_o_k = w_o[0].rearrange("(k p) n -> k p n", p=P)
            sp.dma_start(D_LN1[:, 0, :], ln1_g[0:1, :].partition_broadcast(P)).then_inc(ln1_in, 16)
            sp.dma_start(D_LN1[:, 1, :], ln1_b[0:1, :].partition_broadcast(P)).then_inc(ln1_in, 16)
            for k in range(KD):
                if k >= 2:
                    sp.wait_ge(wo_lo, k - 1)
                sp.dma_start(D_RAW[k % 2], w_o_k[k]).then_inc(wo_raw[k % 2], 16)

            def load_dx(t, s):
                sp.dma_start(D_X[s], xp_t[t]).then_inc(dx_in[s], 16)

            load_dx(0, 0)
            load_dx(1, 1)

            def step_d(t, s):
                sp.wait_ge(d_res, t + 1)
                load_dx(t + 2, s)
                sp.wait_ge(d_x1, t + 1)
                sp.dma_start(x1_t[t], D_X1[s]).then_inc(x1_stored[s], 16)

            with sp.Fori(0, 7) as i:
                for s in range(2):
                    step_d(2 * i + s, s)
            sp.wait_ge(d_res, 15)
            sp.dma_start(D_X[0][0:TS, :], x_sample[0]).then_inc(dx_in[0], 16)
            for t in (14, 15):
                sp.wait_ge(d_x1, t + 1)
                sp.dma_start(x1_t[t], D_X1[t % 2]).then_inc(x1_stored[t % 2], 16)
            sp.wait_ge(d_x1, 17)
            sp.dma_start(x1_dram[SEQ:TOK, :], D_X1[0][0:TS, :]).then_inc(x1_stored[0], 16)
            sp.wait_ge(x1_stored[0], 9 * 16)
            sp.wait_ge(x1_stored[1], 8 * 16)
            sp.wait_ge(d_lo, 17)

            def load_gu(c, n):
                for w in range(2):
                    sp.dma_start(E_GRAW[:, :, w, :], w_gu_c[c, w]).then_inc(gu_raw, 16)

            def load_dn(c, half):
                sp.dma_start(E_DRAW, w_dn_c[c][:, 11 * half:11 * half + 11, :]).then_inc(wd_raw, 16)

            def tile_io(n, load, store):
                if not isinstance(n, int) or n:
                    sp.wait_ge(y_stored, 16 * n)
                load().then_inc(e_x1, 16)
                sp.wait_ge(e_y, n + 1)
                store().then_inc(y_stored, 16)

            def prompt_tile(n):
                tile_io(n, lambda: sp.dma_start(E_X1, x1_t[n]), lambda: sp.dma_start(yp_t[n], E_X1))

            for grp in range(2):
                base = NF * grp
                load_gu(0, base)
                if grp == 0:
                    with sp.Fori(1, NF) as c:
                        sp.wait_ge(gu_lo, c)
                        load_gu(c, c)
                else:
                    sp.wait_ge(gu_lo, 1 + NF)
                    load_gu(1, 1)
                    prompt_tile(0)
                    with sp.Fori(2, 9) as c:
                        sp.wait_ge(gu_lo, c + NF)
                        load_gu(c, c)
                        prompt_tile(c - 1)
                    with sp.Fori(9, NF) as c:
                        sp.wait_ge(gu_lo, c + NF)
                        load_gu(c, c)
                sp.wait_ge(gu_lo, base + NF)
                sp.wait_ge(gu_mm, (44, 110)[grp])
                load_dn(0, 0)
                sp.wait_ge(wd_lo, 16 * grp + 1)
                load_dn(0, 1)
                with sp.Fori(1, KD) as c:
                    for half in range(2):
                        sp.wait_ge(wd_lo, 2 * c + half + 16 * grp)
                        load_dn(c, half)
                if grp == 0:
                    sp.wait_ge(wd_lo, 16)
                    sp.wait_ge(dn_mm, 16)
            with sp.Fori(8, NT) as n:
                prompt_tile(n)
            tile_io(16, lambda: sp.dma_start(E_X1[0:TS, :], x1_dram[SEQ:TOK, :]),
                    lambda: sp.dma_start(y_sample[0], E_X1[0:TS, :]))
            sp.wait_ge(y_stored, 16 * (NT + 1))

        @block.gpsimd
        def _(pool):
            own = Steps(pool, pool_steps)
            own.done(pool.memset(ident[:, :], 1.0))
            own.done(pool.memset(mask_b[:, :], FAR))
            own.wait()
            own.done(pool.affine_select(out=ident[:, :], in_=ident[:, :], compare_op=ALU.is_equal, fill=0.0,
                                        base=0, pattern=[[-1, P]], channel_multiplier=1))
            own.done(pool.affine_select(out=mask_b[:, :], in_=mask_b[:, :], compare_op=ALU.is_ge, fill=0.0,
                                        base=0, pattern=[[1, P]], channel_multiplier=-1))
            own.wait()
            own.done(pool.tensor_copy(ident_b[:, :], ident[:, :]))
            for t in range(HIST):
                own.done(pool.memset(c1(C_INV + t), 1.0 / (t + 1)))
            own.done(pool.memset(c1(C_NEGHALF), -0.5))
            own.done(pool.memset(c1(C_EPS), EPS))
            own.wait()
            pool.memset(B_SEL[0:2, 0, :], 1.0).then_inc(consts_set, 1)

            def rstd(stat):
                own.done(pool.tensor_tensor(stat[:, 14:15], stat[:, 13:14], c1(C_EPS), ALU.add))
                own.wait()
                return pool.tensor_tensor(stat[:, 15:16], stat[:, 14:15], c1(C_NEGHALF), ALU.pow)

            def all_max(dst, src):
                return pool.partition_all_reduce(dst, src, P, RMAX)

            def rstd_a(t, s):
                pool.wait_ge(a_aggr, t + 1)
                rstd(A_STAT[s]).then_inc(a_rstd, 1)

            def lo_a(t, s, rows=P):
                pool.wait_ge(a_hi, t + 1)
                pool.tensor_tensor(hidden_t[:, t, :, 1, 0:rows], A_HF[s].rearrange("p (k t) -> p k t", k=KD)[:, :, 0:rows],
                                   hidden_t[:, t, :, 0, 0:rows], ALU.subtract).then_inc(a_lo, 1)

            rstd_a(0, 0)
            pool.wait_ge(mod_max, 1)
            all_max(small[:, 2:4], small[:, 0:2]).then_inc(mod_ar, 1)

            def four_a(q):
                for s in range(4):
                    rstd_a(4 * q + s + 1, (s + 1) % 2)
                    lo_a(4 * q + s, s % 2)

            own_per = 4
            with pool.Fori(0, 3) as q:
                own.enter(q, 0, own_per)
                four_a(q)
            own.leave(3)
            four_a(3)
            lo_a(16, 0, TS)
            pool.wait_ge(mod_max, 2)
            all_max(small[:, 2:4], small[:, 0:2]).then_inc(mod_ar, 1)

            for c in range(16):
                s = c % 2
                pool.wait_ge(w_mx, c + 1)
                all_max(small[:, 8 + s:9 + s], small[:, 6 + s:7 + s]).then_inc(w_ar, 1)
            pool.wait_ge(fin_max, 1)
            all_max(small[:, 44:48], small[:, 40:44]).then_inc(fin_ar, 1)

            with pool.Fori(0, NPAIR) as hp:
                for u in range(2 * NU):
                    b, kc = UNITS[u % NU]
                    par = u % 2
                    for j in range(4):
                        w = (j + 1) * P if kc == b else BLK
                        z = 8 * NU * hp + 4 * u + j
                        pool.wait_ge(scan_set, z + 1)
                        pool.wait_ge(be_set, z + 1)
                        pool.tensor_tensor(C_A[:, par, j, 0:w], C_A[:, par, j, 0:w],
                                           PRW[:, j, par, 1:w + 1], ALU.mult).then_inc(prod_set, 1)

            def rstd_d(ready, done, n, s):
                pool.wait_ge(ready, n)
                rstd(D_STAT[s]).then_inc(done, 1)

            def lo_d(t, s, rows=P):
                pool.wait_ge(d_hi, t + 1)
                pool.tensor_tensor(hidden_t[:, t, :, 1, 0:rows], D_HF[s].rearrange("p (k t) -> p k t", k=KD)[:, :, 0:rows],
                                   hidden_t[:, t, :, 0, 0:rows], ALU.subtract).then_inc(d_lo, 1)

            rstd_d(d_aggr1, d_rstd1, 1, 0)
            rstd_d(d_aggr2, d_rstd2, 1, 0)

            def two_d(i):
                for s in range(2):
                    t = 2 * i + s
                    rstd_d(d_aggr1, d_rstd1, t + 2, (s + 1) % 2)
                    rstd_d(d_aggr2, d_rstd2, t + 2, (s + 1) % 2)
                    lo_d(t, s)

            with pool.Fori(0, 8) as i:
                own.enter(i, 0, 4)
                two_d(i)
            own.leave(8)
            lo_d(16, 0, TS)

            def lo_hid(m, j, cols, n):
                pool.wait_ge(hid_hi, m + 1)
                pool.tensor_tensor(E_HID[:, j, 1, cols:cols + n], E_H[:, 0:n], E_HID[:, j, 0, cols:cols + n],
                                   ALU.subtract).then_inc(hid_lo, 1)

            def rstd_e(n):
                pool.wait_ge(e_aggr, n + 1)
                rstd(E_STAT).then_inc(e_rstd, 1)

            with pool.Fori(0, NF) as j:
                for blk in range(2):
                    lo_hid(2 * j + blk, j, BLK * blk, BLK)
            with pool.Fori(0, 8) as j:
                own.enter(j, 0, 1)
                for blk in range(3):
                    lo_hid(2 * NF + 3 * j + blk, j, BLK * blk, BLK if blk < 2 else TS)
                rstd_e(j)
            own.leave(8)
            with pool.Fori(8, NF) as j:
                for blk in range(3):
                    lo_hid(2 * NF + 3 * j + blk, j, BLK * blk, BLK if blk < 2 else TS)
            with pool.Fori(8, NT + 1) as n:
                own.enter(n, 8, 1)
                rstd_e(n)
            own.leave(9)

        @block.scalar
        def _(act):
            act.wait_ge(ct_mm, 1)
            act.activation(A_CSIG, ps[:, 6, 0:16], ACT.Sigmoid).then_inc(csig_set, 1)

            def modulate(src_bank, full, t, s, vec, group, done, rows=P):
                for k in range(KD):
                    ins = act.activation(full[:, k * P:k * P + rows],
                                         ps[:, src_bank + k // 4, (k % 4) * P:(k % 4) * P + rows], ACT.Identity,
                                         scale=mod_t[:, vec + 1, k, group:group + 1],
                                         bias=mod_t[:, vec, k, group:group + 1])
                ins.then_inc(done, 1)

            def hi_part(t, full, full_done, hi_done, rows=P):
                act.wait_ge(full_done, t + 1)
                act.activation(hidden_t[:, t, :, 0, 0:rows], full.rearrange("p (k t) -> p k t", k=KD)[:, :, 0:rows],
                               ACT.Identity).then_inc(hi_done, 1)

            def tile_a(t, s, first=False, rows=P, group=0):
                act.wait_ge(a_tr, t + 1)
                if not first:
                    act.wait_ge(a_lo, t - 1)
                modulate(2 * s, A_HF[s], t, s, 0, group, a_full, rows)
                hi_part(t, A_HF[s], a_full, a_hi, rows)

            act.wait_ge(mod_set, 1)
            tile_a(0, 0, True)
            tile_a(1, 1, True)
            with act.Fori(1, 8) as i:
                for s in range(2):
                    tile_a(2 * i + s, s)
            tile_a(16, 0, False, TS, 1)

            def w_split(c, s):
                act.wait_ge(w_s, c + 1)
                act.activation(B_HL[s][:, 0:KD * P], B_RAW[s], ACT.Identity,
                               scale=c1(C_W + 2 * s)).then_inc(w_hi, 1)

            def evac(c, s, dst, prompt_at=0, sample_at=SEQ):
                for blk in range(5):
                    act.wait_ge(proj_mm, 5 * c + blk + 1)
                    n = BLK if blk < 4 else TS
                    at = prompt_at + BLK * blk if blk < 4 else sample_at
                    act.activation(dst[:, at:at + n], ps[:, blk, 0:n], ACT.Identity,
                                   scale=c1(C_W + 2 * s + 1)).then_inc(proj_out, 1)

            def wpool_evac(g):
                for blk in range(5):
                    m = 5 * g + blk
                    act.wait_ge(wpool_mm, m + 1)
                    n = BLK if blk < 4 else TS
                    act.activation(B_S[g % 2][:, BLK * blk:BLK * blk + n], ps[:, 5 + m % 2, 0:n], ACT.Identity,
                                   scale=c1(C_PSCALE + g)).then_inc(wpool_out, 1)

            act.wait_ge(misc_in, 64)
            w_split(0, 0)
            for g in range(4):
                w_split(g + 1, (g + 1) % 2)
                if g:
                    act.wait_ge(pooled_set, g)
                    act.wait_ge(npool_mm, g)
                evac(g, g % 2, B_U, 16, 2080)
                if g:
                    wpool_evac(g - 1)
            for u in range(2):
                w_split(5 + u, 1 - u)
                evac(4 + u, u, B_BIG[:, TOK * u:TOK * (u + 1)])
            for u in range(2):
                w_split(7 + u, 1 - u)
                act.wait_ge(q_stored[u], 16)
                evac(6 + u, u, B_BIG[:, TOK * u:TOK * (u + 1)])
            wpool_evac(3)
            for s in range(2):
                w_split(9 + s, 1 - s)
                if s == 0:
                    act.wait_ge(rmax_set, 4)
                    act.wait_ge(pool_stored, 64)
                evac(8 + s, s, B_VT[s])
            for c in range(10, 16):
                s = c % 2
                if c < 15:
                    w_split(c + 1, 1 - s)
                act.wait_ge(kvt_mm, 5 * (c - 9))
                if c < 12:
                    act.wait_ge(k_stored[s], 16)
                elif c < 14:
                    act.wait_ge(k_stored[s], 32)
                else:
                    act.wait_ge(vmax_set, c - 13)
                evac(c, s, B_VT[s])

            def sigmoids(hp, u):
                b, kc = UNITS[u % NU]
                par = u % 2
                for j in range(4):
                    z = 8 * NU * hp + 4 * u + j
                    w = (j + 1) * P if kc == b else BLK
                    act.wait_ge(z_mm, z + 1)
                    if u >= 1:
                        act.wait_ge(scan_set, z - 3)
                    if u >= 2:
                        act.wait_ge(prod_set, z - 7)
                    act.activation(PRW[:, j, par, 0:w], ps[:, j, 0:w], ACT.Sigmoid, scale=-SCALE).then_inc(sg_set, 1)
                    if u >= 2 and j == 0:
                        act.wait_ge(at_mm, 8 * NU * hp + 4 * u - 4)
                    act.activation(C_A[:, par, j, 0:w], ps[:, j, 0:w], ACT.Sigmoid, scale=SCALE).then_inc(be_set, 1)

            def evac_at(hp, u):
                b, kc = UNITS[u % NU]
                for kt in (0, 2):
                    j0 = kt * P if kc == b else 0
                    m = 8 * NU * hp + 4 * u + kt
                    act.wait_ge(at_mm, m + 1)
                    if u >= 1:
                        act.wait_ge(av_mm, m - 3)
                    act.activation(C_AT[kt][:, j0:BLK], ps[:, 4, j0:BLK], ACT.Identity).then_inc(at_act, 1)

            with act.Fori(0, NPAIR) as hp:
                for u in range(2 * NU):
                    sigmoids(hp, u)
                    if u:
                        evac_at(hp, u - 1)
                evac_at(hp, 2 * NU - 1)
            for g in range(2):
                act.wait_ge(sz_mm, g + 1)
                for dst, sc in ((C_SP[g], -SCALE), (C_SA[g], SCALE)):
                    act.activation(dst[:, 0:PAST], ps[:, 2 * g, 0:PAST], ACT.Sigmoid, scale=sc).then_inc(ssig, 1)
                    act.activation(dst[:, PAST:PAST + TS], ps[:, 2 * g + 1, 0:TS], ACT.Sigmoid, scale=sc).then_inc(ssig, 1)

            for k in range(KD):
                act.wait_ge(wo_raw[k % 2], 16 * (k // 2 + 1))
                act.activation(D_WO[:, 0, k, :], D_RAW[k % 2], ACT.Identity, scale=c1(C_SWO)).then_inc(wo_hi, 1)

            def tile_d(t, s, first=False, rows=P, group=0):
                act.wait_ge(d_tr, t + 1)
                if not first:
                    act.wait_ge(d_lo, t - 1)
                modulate(4 + 2 * s, D_HF[s], t, s, 2, group, d_full, rows)
                hi_part(t, D_HF[s], d_full, d_hi, rows)

            tile_d(0, 0, True)
            tile_d(1, 1, True)
            with act.Fori(1, 8) as i:
                for s in range(2):
                    tile_d(2 * i + s, s)
            tile_d(16, 0, False, TS, 1)

            def gu_split(n, s, used):
                act.wait_ge(gu_raw, 32 * (n + 1))
                if used is not None:
                    act.wait_ge(gu_mm, used)
                act.activation(E_GHL[s][:, 0, :, :, :], E_GRAW, ACT.Identity, scale=c1(C_SGU)).then_inc(gu_hi, 1)

            def hidden(m, j, blk, cols, n):
                act.wait_ge(gu_mm, m + 1)
                if blk < 2:
                    gate = ps[:, 2 * blk, 0:n]
                else:
                    gate = ps[:, 4, 0:n]
                if not isinstance(m, int) or m:
                    act.wait_ge(hid_set, m)
                act.activation(E_SIG[:, 0:n], gate, ACT.Sigmoid, scale=c1(C_F1)).then_inc(sig_set, 1)
                act.wait_ge(hid_set, m + 1)
                act.activation(E_HID[:, j, 0, cols:cols + n], E_H[:, 0:n], ACT.Identity).then_inc(hid_hi, 1)

            def dn_split(n, h, s, used):
                act.wait_ge(wd_raw, 16 * (n + 1))
                if used is not None:
                    act.wait_ge(dn_mm, used)
                act.activation(E_DHL[s][:, 0, 11 * h:11 * h + 11, :], E_DRAW, ACT.Identity,
                               scale=c1(C_SWD)).then_inc(wd_hi, 1)

            def dn_evac(m, c, grp, blk):
                act.wait_ge(dn_mm, m + 1)
                if blk < 2:
                    dst = hidden_t[:, 8 * grp + 4 * blk:8 * grp + 4 * blk + 4, :, :, :].bitcast(f32).rearrange(
                        "p i k a t -> p i (k a t)")
                    act.activation(dst[:, :, bass.ds(c * P, P)], bank((0, 1, 4)[blk], BLK, 0), ACT.Identity,
                                   scale=mod_t[:, 4, bass.ds(c, 1), 0:1].rearrange("p a b -> p (a b)")).then_inc(dn_out, 1)
                else:
                    dst = hidden_t[:, NT, :, :, :].bitcast(f32).rearrange("p k a t -> p (k a t)")
                    act.activation(dst[:, bass.ds(c * P, TS)], ps[:, 4, 0:TS], ACT.Identity,
                                   scale=mod_t[:, 4, bass.ds(c, 1), 1:2].rearrange("p a b -> p (a b)")).then_inc(dn_out, 1)

            for grp in range(2):
                nb = 2 + grp
                m0, n0 = 2 * NF * grp, NF * grp
                d0, h0 = 16 * grp, 16 * grp

                def chunk(j, s, last=False):
                    if not last:
                        gu_split(n0 + j + 1, 1 - s, m0 + nb * j if not isinstance(j, int) or j else None)
                    for blk in range(nb):
                        hidden(m0 + nb * j + blk, j, blk, BLK * blk, BLK if blk < 2 else TS)

                gu_split(n0, 0, None)
                chunk(0, 0)
                chunk(1, 1)
                with act.Fori(1, NF // 2 - 1) as i:
                    for s in range(2):
                        chunk(2 * i + s, s)
                chunk(NF - 2, 0)
                chunk(NF - 1, 1, True)
                for h in range(2):
                    dn_split(h0 + h, h, 0, None)

                def down(c, s, last=False):
                    if not last:
                        for h in range(2):
                            dn_split(h0 + 2 * (c + 1) + h, h, 1 - s,
                                     d0 + nb * c if not isinstance(c, int) or c else None)
                    for blk in range(nb):
                        dn_evac(d0 + nb * c + blk, c, grp, blk)

                down(0, 0)
                down(1, 1)
                with act.Fori(1, 3) as i:
                    for s in range(2):
                        down(2 * i + s, s)
                down(6, 0)
                down(7, 1, True)

        @block.vector
        def _(v):
            own = Steps(v, dve)

            def step(ins):
                own.done(ins)
                own.wait()

            def pow2(src, s, f, n=1):
                t, e2, inv = small[:, 48:48 + n], small[:, 52:52 + n], small[:, 56:56 + n]
                step(v.tensor_scalar(t, src, 1e-30, 1e36, ALU.max, ALU.min))
                step(v.tensor_scalar(e2.bitcast(i32), t.bitcast(i32), 0x7F800000, None, ALU.bitwise_and))
                step(v.tensor_scalar(inv.bitcast(i32), e2.bitcast(i32), -1.0, float(0x7F000000), ALU.mult, ALU.add))
                own.done(v.tensor_scalar(s, inv, 2.0 ** TOP, None, ALU.mult))
                step(v.tensor_scalar(f, e2, 2.0 ** -TOP, None, ALU.mult))

            def abs_max(dst, src):
                return v.tensor_reduce(dst, src, AX.X, ALU.max, apply_absolute_value=True)

            def stats(x, stat, rows, aggr):
                own.done(v.bn_stats(stat[0:rows, 0:6], x[0:rows, 0:512]))
                step(v.bn_stats(stat[0:rows, 6:12], x[0:rows, 512:1024]))
                v.memset(small[:, 64:65], 0.0)
                v.bn_aggr(stat[0:rows, 12:14], stat[0:rows, 0:12]).then_inc(aggr, 1)

            def ln_a(t, s, first=False, rows=P):
                v.wait_ge(x_in[s], 16 * ((t - s) // 2 + 1) if isinstance(t, int) else t * 8 + 16 - 8 * s)
                stats(A_X[s], A_STAT[s], rows, a_aggr)
                v.wait_ge(a_rstd, t + 1)
                if not first:
                    v.wait_ge(a_tr, t - 1)
                v.tensor_scalar(A_XH[s][0:rows, :], A_X[s][0:rows, :], A_STAT[s][0:rows, 12:13],
                                A_STAT[s][0:rows, 15:16], ALU.subtract, ALU.mult).then_inc(a_xhat, 1)

            for s in range(2):
                own.done(v.memset(A_STAT[s], 1.0))
            step(v.memset(D_G1ROW[0:2, :], 0.0))
            ln_a(0, 0, True)
            v.wait_ge(csig_set, 1)
            v.tensor_tensor(A_CT, ps[:, 6, 0:16], A_CSIG, ALU.mult).then_inc(ct_set, 1)
            v.wait_ge(brow_in, 32)

            def ada(j, s):
                v.wait_ge(ada_mm, j + 1)
                v.tensor_tensor(A_MROW[0:2, bass.ds(512 * j, 512)], ps[0:2, 4 + s, :],
                                A_BROW[0:2, bass.ds(512 * j, 512)], ALU.add).then_inc(ada_row, 1)

            def finish_mod(n, vec, s_col, f_col, bound):
                v.wait_ge(modt_mm, n)
                nv = 2 if n == 1 else 3
                src = ps[:, 6, 0:16 * nv].rearrange("p (v k b) -> p v k b", v=nv, k=KD)
                own.done(v.tensor_copy(mod_t[:, vec, :, :], src[:, 0, :, :]))
                if nv == 3:
                    own.done(v.tensor_copy(mod_t[:, 4, :, :], src[:, 2, :, :]))
                step(v.tensor_scalar(mod_t[:, vec + 1, :, :], src[:, 1, :, :], 1.0, None, ALU.add))
                flat = [mod_t[:, vec + i, :, :].rearrange("p k b -> p (k b)") for i in range(2)]
                own.done(abs_max(small[:, 0:1], flat[0]))
                abs_max(small[:, 1:2], flat[1]).then_inc(mod_max, 1)
                v.wait_ge(mod_ar, n)
                step(v.tensor_tensor(small[:, 4:5], small[:, 2:3], small[:, 3:4], ALU.add))
                step(v.tensor_scalar(c1(bound), small[:, 4:5], LN_ROOT, None, ALU.mult))
                pow2(c1(bound), c1(s_col), c1(f_col))
                own.done(v.tensor_scalar(flat[0], flat[0], c1(s_col), None, ALU.mult))
                v.tensor_scalar(flat[1], flat[1], c1(s_col), None, ALU.mult).then_inc(mod_set, 1)

            for j in range(4):
                ada(j, j % 2)
            finish_mod(1, 0, C_SH, C_FH, C_BOUND)
            ln_a(1, 1, True)
            ln_a(2, 0)
            ada(4, 0)
            ln_a(3, 1)
            ln_a(4, 0)
            ada(5, 1)
            with v.Fori(1, 4) as q:
                own.enter(q, 1, 8)
                for u in range(2):
                    ln_a(4 * q + 2 * u + 1, 1)
                    if u == 0:
                        ln_a(4 * q + 2, 0)
                    else:
                        ln_rows_next = 4 * q + 4
                        v.wait_ge(x_in[0], 8 * ln_rows_next + 16)
                        stats(A_X[0], A_STAT[0], P, a_aggr)
                        v.wait_ge(a_rstd, ln_rows_next + 1)
                        v.wait_ge(a_tr, ln_rows_next - 1)
                        v.tensor_scalar(A_XH[0], A_X[0], A_STAT[0][:, 12:13], A_STAT[0][:, 15:16],
                                        ALU.subtract, ALU.mult).then_inc(a_xhat, 1)
                    ada(4 + 2 * q + u, u)
            own.leave(3)
            v.wait_ge(modt_mm, 2)
            own.done(v.tensor_copy(D_G1ROW[0:2, :], A_MROW[0:2, 2 * D:3 * D]))
            v.wait_ge(consts_set, 1)
            step(v.tensor_scalar(B_SEL[0:2, 1, :], B_SEL[0:2, 0, :], ident[0:2, 1:2], None, ALU.mult))
            step(v.tensor_scalar(B_SEL[0:2, 0, :], B_SEL[0:2, 0, :], ident[0:2, 0:1], None, ALU.mult))
            finish_mod(2, 2, C_SH2, C_FH2, C_BOUND + 1)
            v.wait_ge(hist_mm, 1)
            step(v.tensor_copy(HIST_T, ps[:, 7, 0:4 * HIST]))

            def prep(c):
                s = c % 2
                v.wait_ge(w_in_raw[s], 16 * (c // 2 + 1))
                if c >= 2:
                    v.wait_ge(proj_out, 5 * (c - 1))
                abs_max(small[:, 6 + s:7 + s], B_RAW[s]).then_inc(w_mx, 1)
                v.wait_ge(w_ar, c + 1)
                pow2(small[:, 8 + s:9 + s], c1(C_W + 2 * s), c1(C_W + 2 * s + 1))
                v.tensor_tensor(c1(C_W + 2 * s + 1), c1(C_W + 2 * s + 1), c1(C_FH), ALU.mult).then_inc(w_s, 1)
                v.wait_ge(w_hi, c + 1)
                v.scalar_tensor_tensor(B_HL[s][:, KD * P:2 * KD * P], B_RAW[s], c1(C_W + 2 * s),
                                       B_HL[s][:, 0:KD * P], ALU.mult, ALU.subtract).then_inc(w_lo, 1)

            def pool_rows(g):
                win = 2 ** (g + 1)
                v.wait_ge(proj_out, 5 * (g + 1))
                step(v.tensor_copy(B_U[:, 2065:2080], HIST_T[:, HIST * g:HIST * (g + 1)]))
                if g:
                    v.wait_ge(pool_stored, 16 * g)
                src = B_U
                for i in range(g + 1):
                    d, dst = 2 ** i, B_S[i % 2]
                    st = 2 * d - 1
                    step(v.tensor_tensor(dst[:, st:UW], src[:, st:UW], src[:, st - d:UW - d], ALU.add))
                    src = dst
                dst = B_S[(g + 1) % 2]
                first = 16 + win - 1
                own.done(v.scalar_tensor_tensor(dst[:, first:UW], src[:, first:UW], 1.0 / win,
                                                B_U[:, first:UW], ALU.mult, ALU.subtract))
                step(v.tensor_tensor(dst[:, 16:first], src[:, 16:first], c1(C_INV, win - 1), ALU.mult))
                v.tensor_tensor(dst[:, 16:first], dst[:, 16:first], B_U[:, 16:first],
                                ALU.subtract).then_inc(pooled_set, 1)

            def last_rows(g):
                v.wait_ge(npool_mm, g + 1)
                v.tensor_copy(B_NPOOL[0:HIST, :].rearrange("p (b n) -> p b n", b=2)[:, :, g * P:(g + 1) * P],
                              ps[0:HIST, 7, 0:2 * P].rearrange("p (b n) -> p b n", b=2)).then_inc(npool_out, 1)

            def pool_max(g):
                v.wait_ge(wpool_out, 5 * (g + 1))
                abs_max(c1(C_POOLMAX + g), B_S[g % 2][:, 0:TOK]).then_inc(rmax_set, 1)

            def rows_out(c):
                for g in range(5):
                    m = 5 * (c - 8) + g
                    slot = m % 2
                    v.wait_ge(kvt_mm, m + 1)
                    if m >= 2:
                        v.wait_ge(kv_stored[slot], 16 * (m // 2))
                    n, rows = (BLK, P) if g < 4 else (P, TS)
                    v.tensor_copy(B_STG[slot][0:rows, 0:n], ps[0:rows, 5 + slot, 0:n]).then_inc(kvt_out, 1)

            def big_max(c):
                v.wait_ge(big_in, 48 * (c + 1))
                for i, (_, at, n) in enumerate(BIGS):
                    ins = abs_max(small[:, 16 + 8 * i + c:17 + 8 * i + c], B_BIG[:, at:at + n])
                ins.then_inc(big_mx, 1)

            own.done(v.memset(B_U[:, 0:16], 0.0))
            step(v.memset(B_U[:, 2064:2065], 0.0))
            prep(0)
            for c in range(16):
                if c < 15:
                    prep(c + 1)
                if 1 <= c <= 3:
                    pool_max(c - 1)
                if c < 4:
                    pool_rows(c)
                    last_rows(c)
                if c == 8:
                    pool_max(3)
                if c >= 8:
                    rows_out(c)
                    big_max(c - 8)
                if c >= 12:
                    v.wait_ge(proj_out, 5 * (c + 1))
                    abs_max(c1(C_VMAX + c - 12), B_VT[c % 2]).then_inc(vmax_set, 1)
            v.wait_ge(cv_in, 16)
            step(abs_max(c1(C_VMAX + 4), B_CV))
            v.wait_ge(vmax_set, 4)
            v.wait_ge(big_mx, 8)
            v.wait_ge(rmax_set, 4)
            own.done(v.tensor_reduce(small[:, 40:43], small[:, 16:40].rearrange("p (i c) -> p i c", i=3),
                                     AX.X, ALU.max))
            v.tensor_reduce(small[:, 43:44], c1(C_POOLMAX, 9), AX.X, ALU.max).then_inc(fin_max, 1)
            v.wait_ge(fin_ar, 1)
            pow2(small[:, 44:48], c1(C_SGU, 4), c1(C_FGU, 4), 4)
            step(v.tensor_tensor(small[:, 60:61], c1(C_BOUND + 1), small[:, 44:45], ALU.mult))
            step(v.tensor_scalar(small[:, 61:62], small[:, 60:61], LN_ROOT, None, ALU.mult))
            step(v.tensor_tensor(small[:, 62:63], small[:, 61:62], small[:, 61:62], ALU.mult))
            pow2(small[:, 62:63], c1(C_SHID), c1(C_FHID))
            own.done(v.tensor_tensor(c1(C_FWOMIX), c1(C_FWO), c1(C_FMIX), ALU.mult))
            own.done(v.tensor_tensor(c1(C_FDOWN), c1(C_FWD), c1(C_FHID), ALU.mult))
            step(v.tensor_tensor(c1(C_F1), c1(C_FGU), c1(C_FH2), ALU.mult))
            own.done(v.tensor_tensor(c1(C_F2), c1(C_F1), c1(C_SHID), ALU.mult))
            g2 = mod_t[:, 4, :, :].rearrange("p k b -> p (k b)")
            v.tensor_scalar(g2, g2, c1(C_FDOWN), None, ALU.mult).then_inc(fin_set, 1)
            v.wait_ge(fin_set, 1)

            for g in range(4):
                v.wait_ge(pool_back, 16 * (g + 1))
                parts = [(C_POOL[:, 0:SEQ].rearrange("p (i t) -> p i t", t=P),
                          [hidden_t[:, 0:NT, g, h, :] for h in range(2)]),
                         (C_POOL[:, SEQ:TOK], [hidden_t[:, NT, g, h, 0:TS] for h in range(2)])]
                for src, (hi, lo) in parts:
                    step(v.tensor_scalar(hi, src, c1(C_SMIX), None, ALU.mult))
                for n, (src, (hi, lo)) in enumerate(parts):
                    ins = v.scalar_tensor_tensor(lo, src, c1(C_SMIX), hi, ALU.mult, ALU.subtract)
                    if n == 0:
                        own.done(ins)
                ins.then_inc(pool_split, 1)

            def scans(hp, u):
                b, kc = UNITS[u % NU]
                par = u % 2
                if kc == b:
                    step(v.memset(C_PR[:, par * PB + P:par * PB + P + 3 * (2 * PB + P) + 1:2 * PB + P], 1.0))
                for j in range(4):
                    z = 8 * NU * hp + 4 * u + j
                    w = (j + 1) * P if kc == b else BLK
                    v.wait_ge(sg_set, z + 1)
                    row = PRW[:, j, par, w - 1::-1] if w < PB else None
                    v.tensor_tensor_scan(row, row, row, PRW[:, j, par, w:w + 1],
                                         ALU.mult, ALU.bypass).then_inc(scan_set, 1)
                v.wait_ge(scan_set, 8 * NU * hp + 4 * u + 4)
                if u:
                    v.wait_ge(prod_set, 8 * NU * hp + 4 * u)
                step(v.tensor_copy(PRW[:, :, 1 - par, BLK:BLK + 1], PRW[:, :, par, 0:1]))

            def evac_at_dve(hp, u):
                b, kc = UNITS[u % NU]
                for kt in (1, 3):
                    j0 = kt * P if kc == b else 0
                    m = 8 * NU * hp + 4 * u + kt
                    v.wait_ge(at_mm, m + 1)
                    if u >= 1:
                        v.wait_ge(av_mm, m - 3)
                    v.tensor_copy(C_AT[kt][:, j0:BLK], ps[:, 5, j0:BLK]).then_inc(at_dve, 1)
                if kc == 0:
                    e = u // NU
                    r = slice(HD * e, HD * e + HD)
                    ob = 8 * hp + 4 * e + b
                    v.wait_ge(av_mm, 8 * NU * hp + 4 * u + 4)
                    v.tensor_scalar(C_ST[b % 2][r, :], ps[r, 6 + b % 2, :], c1(C_SMIX)[r, :], None,
                                    ALU.mult).then_inc(o_scaled, 1)
                    v.wait_ge(o_scaled, ob + 1)
                    st = C_ST[b % 2][r, :].rearrange("p (i t) -> p i t", t=P)
                    dst = [hidden_t[r, 4 * b:4 * b + 4, 4 + hp, h, :] for h in range(2)]
                    step(v.tensor_copy(dst[0], st))
                    v.tensor_tensor(dst[1], st, dst[0], ALU.subtract).then_inc(o_split, 1)

            with v.Fori(0, NPAIR) as hp:
                own.enter(hp, 0, 36)
                for u in range(2 * NU):
                    scans(hp, u)
                    if u:
                        evac_at_dve(hp, u - 1)
                evac_at_dve(hp, 2 * NU - 1)
            own.leave(NPAIR)

            for hp in range(NPAIR):
                v.wait_ge(ck_mm, hp + 1)
                v.tensor_copy(C_CKT[:, hp, :], ps[:, 4 + hp % 2, :]).then_inc(ck_set, 1)
            W1 = PAST + TS
            for g in range(2):
                step(v.memset(C_SP[g][:, W1:W1 + 1], 1.0))
                v.wait_ge(ssig, 4 * (g + 1))
                row = C_SP[g][:, W1 - 1::-1]
                step(v.tensor_tensor_scan(row, row, row, 1.0, ALU.mult, ALU.bypass))
                v.tensor_tensor(C_SA[g][:, 0:W1], C_SA[g][:, 0:W1], C_SP[g][:, 1:W1 + 1],
                                ALU.mult).then_inc(sprod, 1)
            for g in range(2):
                v.wait_ge(sat_mm, g + 1)
                v.tensor_copy(C_SAT[g][:, 0:512], ps[:, 4 + g, :]).then_inc(sat_set, 1)
                v.tensor_copy(C_SAT[g][0:TS, 512:640], ps[0:TS, 6 + g, 0:P]).then_inc(sat_set, 1)
            v.wait_ge(so_mm, 1)
            step(v.tensor_scalar(C_SST, ps[:, 0, 0:P], c1(C_SMIX), None, ALU.mult))
            st = C_SST.rearrange("p (h t) -> p h t", h=4)
            step(v.tensor_copy(hidden_t[:, NT, 4:8, 0, 0:TS], st))
            v.tensor_tensor(hidden_t[:, NT, 4:8, 1, 0:TS], st, hidden_t[:, NT, 4:8, 0, 0:TS],
                            ALU.subtract).then_inc(so_split, 1)

            for b in range(2):
                for n in range(2):
                    v.wait_ge(g1_mm, 2 * b + n + 1)
                    v.tensor_scalar(D_G1[:, b, 512 * n:512 * (n + 1)], ps[:, 4 + 2 * b + n, :], c1(C_FWOMIX), None,
                                    ALU.mult).then_inc(g1_set, 1)
            for k in range(KD):
                v.wait_ge(wo_hi, k + 1)
                v.scalar_tensor_tensor(D_WO[:, 1, k, :], D_RAW[k % 2], c1(C_SWO), D_WO[:, 0, k, :],
                                       ALU.mult, ALU.subtract).then_inc(wo_lo, 1)
            v.wait_ge(ln1_in, 32)
            v.wait_ge(g1_set, 4)
            for s in range(2):
                own.done(v.memset(D_STAT[s], 1.0))
            own.wait()

            def tile_d(t, s, xin, first=False, rows=P, group=0):
                r = slice(0, rows)
                stat = D_STAT[s]
                v.wait_ge(d_mm, t + 1)
                v.tensor_tensor(D_R[s][r, :], ps[r, 2 * s:2 * s + 2, :].rearrange("p a n -> p (a n)"),
                                D_G1[r, group, :], ALU.mult).then_inc(d_mo, 1)
                v.wait_ge(d_mo, t + 1)
                v.wait_ge(dx_in[s], xin)
                v.scalar_tensor_tensor(D_R[s][r, :], D_X[s][r, :], ALPHA, D_R[s][r, :],
                                       ALU.mult, ALU.add).then_inc(d_res, 1)
                v.wait_ge(d_res, t + 1)
                stats(D_R[s], stat, rows, d_aggr1)
                v.wait_ge(d_rstd1, t + 1)
                step(v.scalar_tensor_tensor(D_R[s][r, :], D_R[s][r, :], stat[r, 12:13], D_LN1[r, 0, :],
                                            ALU.subtract, ALU.mult))
                if not first:
                    v.wait_ge(x1_stored[s], xin - 16)
                    v.wait_ge(d_tr, t - 1)
                v.scalar_tensor_tensor(D_X1[s][r, :], D_R[s][r, :], stat[r, 15:16], D_LN1[r, 1, :],
                                       ALU.mult, ALU.add).then_inc(d_x1, 1)
                v.wait_ge(d_x1, t + 1)
                stats(D_X1[s], stat, rows, d_aggr2)
                v.wait_ge(d_rstd2, t + 1)
                v.tensor_scalar(D_XH[s][r, :], D_X1[s][r, :], stat[r, 12:13], stat[r, 15:16],
                                ALU.subtract, ALU.mult).then_inc(d_xhat, 1)

            tile_d(0, 0, 16, True)
            tile_d(1, 1, 16, True)
            with v.Fori(1, 8) as i:
                own.enter(i, 1, 10)
                for s in range(2):
                    tile_d(2 * i + s, s, 16 * i + 16)
            own.leave(7)
            tile_d(16, 0, 144, False, TS, 1)

            v.wait_ge(misc_in, 64)

            def gu_low(n, s):
                v.wait_ge(gu_hi, n + 1)
                v.scalar_tensor_tensor(E_GHL[s][:, 1, :, :, :].rearrange("p k w n -> p (k w n)"),
                                       E_GRAW.rearrange("p k w n -> p (k w n)"), c1(C_SGU),
                                       E_GHL[s][:, 0, :, :, :].rearrange("p k w n -> p (k w n)"),
                                       ALU.mult, ALU.subtract).then_inc(gu_lo, 1)

            def hidden(m, blk, n):
                gate = ps[:, 2 * blk, 0:n] if blk < 2 else ps[:, 4, 0:n]
                up = ps[:, 2 * blk + 1, 0:n] if blk < 2 else ps[:, 4, TS:2 * TS]
                v.wait_ge(sig_set, m + 1)
                step(v.scalar_tensor_tensor(E_T[:, 0:n], gate, c1(C_F1), E_SIG[:, 0:n], ALU.mult, ALU.mult))
                if not isinstance(m, int) or m:
                    v.wait_ge(hid_lo, m)
                v.scalar_tensor_tensor(E_H[:, 0:n], up, c1(C_F2), E_T[:, 0:n],
                                       ALU.mult, ALU.mult).then_inc(hid_set, 1)

            def ln2(n, rows=P):
                r = slice(0, rows)
                v.wait_ge(e_x1, 16 * (n + 1))
                v.wait_ge(e_tr, n + 1)
                v.scalar_tensor_tensor(E_X1[r, :], E_X1[r, :], ALPHA,
                                       ps[r, 5:7, :].rearrange("p a n -> p (a n)"), ALU.mult, ALU.add).then_inc(e_res, 1)
                v.wait_ge(e_res, n + 1)
                stats(E_X1, E_STAT, rows, e_aggr)
                v.wait_ge(e_rstd, n + 1)
                step(v.scalar_tensor_tensor(E_X1[r, :], E_X1[r, :], E_STAT[r, 12:13], ln2_rows[r, 0, :],
                                            ALU.subtract, ALU.mult))
                v.scalar_tensor_tensor(E_X1[r, :], E_X1[r, :], E_STAT[r, 15:16], ln2_rows[r, 1, :],
                                       ALU.mult, ALU.add).then_inc(e_y, 1)

            def dn_low(n, h, s):
                v.wait_ge(wd_hi, n + 1)
                parts = [E_DHL[s][:, i, 11 * h:11 * h + 11, :].rearrange("p j n -> p (j n)") for i in range(2)]
                v.scalar_tensor_tensor(parts[1], E_DRAW.rearrange("p j n -> p (j n)"), c1(C_SWD), parts[0],
                                       ALU.mult, ALU.subtract).then_inc(wd_lo, 1)

            step(v.memset(E_STAT, 1.0))
            for grp in range(2):
                nb = 2 + grp
                m0, n0, h0 = 2 * NF * grp, NF * grp, 16 * grp

                def chunk(j, s, last=False, with_ln=False):
                    if not last:
                        gu_low(n0 + j + 1, 1 - s)
                    for blk in range(nb):
                        hidden(m0 + nb * j + blk, blk, BLK if blk < 2 else TS)
                    if with_ln:
                        ln2(j)

                gu_low(n0, 0)
                chunk(0, 0, False, grp == 1)
                chunk(1, 1, False, grp == 1)
                if grp == 0:
                    with v.Fori(1, NF // 2 - 1) as i:
                        own.enter(i, 1, 4)
                        for s in range(2):
                            chunk(2 * i + s, s)
                    own.leave(NF // 2 - 2)
                else:
                    with v.Fori(1, 4) as i:
                        own.enter(i, 1, 12)
                        for s in range(2):
                            chunk(2 * i + s, s, False, True)
                    own.leave(3)
                    with v.Fori(4, NF // 2 - 1) as i:
                        own.enter(i, 4, 6)
                        for s in range(2):
                            chunk(2 * i + s, s)
                    own.leave(NF // 2 - 5)
                chunk(NF - 2, 0)
                chunk(NF - 1, 1, True)
                with v.Fori(0, KD // 2) as i:
                    for s in range(2):
                        for h in range(2):
                            dn_low(h0 + 4 * i + 2 * s + h, h, s)
            with v.Fori(8, NT) as n:
                own.enter(n, 8, 3)
                ln2(n)
            own.leave(8)
            ln2(16, TS)

        @block.tensor
        def _(pe):
            pe.wait_ge(consts_set, 1)
            pe.wait_ge(crow_in, 32)
            pe.transpose(ps[:, 6, 0:16], A_CROW[0:16, :], ident[0:16, 0:16]).then_inc(ct_mm, 1)
            ct = A_CT.rearrange("p (b k) -> p b k", b=2)

            def ada(j, s, arrived, first=False):
                pe.wait_ge(wada_in[s], arrived)
                if not first:
                    pe.wait_ge(ada_row, j - 1)
                for k in range(KD):
                    mm = pe.matmul(ps[0:2, 4 + s, :], ct[:, :, k], A_WADA[:, s, k, :], start=(k == 0), stop=(k == KD - 1))
                mm.then_inc(ada_mm, 1)

            def mod_cols(first_row, vecs):
                for i, vec in enumerate(vecs):
                    for k in range(KD):
                        mm = pe.transpose(ps[:, 6, (KD * i + k) * 2:(KD * i + k) * 2 + 2],
                                          A_MROW[0:2, D * vec + P * k:D * vec + P * (k + 1)], ident[0:2, 0:2])
                mm.then_inc(modt_mm, 1)

            def turn(t, s, src, ready, done, bank0, free, first=False, rows=P):
                pe.wait_ge(ready, t + 1)
                if not first:
                    pe.wait_ge(free, t - 1)
                for k in range(KD):
                    mm = pe.transpose(ps[:, bank0 + 2 * s + k // 4, (k % 4) * P:(k % 4) * P + rows],
                                      src[s][0:rows, k * P:(k + 1) * P], ident[0:rows, 0:rows])
                mm.then_inc(done, 1)

            pe.wait_ge(ct_set, 1)
            ada(0, 0, 16, True)
            ada(1, 1, 16, True)
            ada(2, 0, 32)
            ada(3, 1, 32)
            pe.wait_ge(ada_row, 4)
            mod_cols(0, (0, 1))
            turn(0, 0, A_XH, a_xhat, a_tr, 0, a_full, True)
            turn(1, 1, A_XH, a_xhat, a_tr, 0, a_full, True)
            ada(4, 0, 48)
            turn(2, 0, A_XH, a_xhat, a_tr, 0, a_full)
            turn(3, 1, A_XH, a_xhat, a_tr, 0, a_full)
            ada(5, 1, 48)
            with pe.Fori(1, 4) as q:
                for u in range(2):
                    for s in range(2):
                        turn(4 * q + 2 * u + s, s, A_XH, a_xhat, a_tr, 0, a_full)
                    ada(4 + 2 * q + u, u, 16 * q + 48)
            pe.wait_ge(hist_in, 16)
            for g in range(4):
                mm = pe.transpose(ps[:, 7, HIST * g:HIST * (g + 1)], A_HISTROW[0:HIST, P * g:P * (g + 1)],
                                  ident[0:HIST, 0:HIST])
            mm.then_inc(hist_mm, 1)
            turn(16, 0, A_XH, a_xhat, a_tr, 0, a_full, False, TS)
            pe.wait_ge(ada_row, 12)
            mod_cols(1, (3, 4, 5))

            pe.wait_ge(a_hi, NT + 1)
            pe.wait_ge(a_lo, NT + 1)
            pe.wait_ge(a_full, NT + 1)

            def project(c, s, first=False):
                pe.wait_ge(w_hi, c + 1)
                pe.wait_ge(w_lo, c + 1)
                for blk in range(5):
                    if not first:
                        pe.wait_ge(proj_out, 5 * c + blk - 4)
                    n = BLK if blk < 4 else TS
                    for k in range(KD):
                        for wh, xh in TERMS:
                            mm = pe.matmul(bank(blk, n, blk), B_HL[s][:, wh * KD * P + k * P:wh * KD * P + (k + 1) * P],
                                           moving(k, xh, blk), start=(k == 0 and (wh, xh) == (0, 0)),
                                           stop=(k == KD - 1 and (wh, xh) == TERMS[-1]))
                    mm.then_inc(proj_mm, 1)

            def mix_pool(g):
                pe.wait_ge(pooled_set, g + 1)
                for blk in range(5):
                    m = 5 * g + blk
                    if m >= 2:
                        pe.wait_ge(wpool_out, m - 1)
                    at, n = (16 + BLK * blk, BLK) if blk < 4 else (2080, TS)
                    pe.matmul(ps[:, 5 + m % 2, 0:n], B_WPOOL[:, g * P:(g + 1) * P],
                              B_S[(g + 1) % 2][:, at:at + n], start=True, stop=True).then_inc(wpool_mm, 1)

            def last_rows(g):
                pe.wait_ge(proj_out, 5 * (g + 1))
                if g:
                    pe.wait_ge(npool_out, g)
                for b, at in enumerate((16 + SEQ - HIST, 2080 + TS - HIST)):
                    mm = pe.transpose(ps[0:HIST, 7, b * P:(b + 1) * P], B_U[:, at:at + HIST], ident[:, :])
                mm.then_inc(npool_mm, 1)

            def token_rows(c, s):
                for g in range(5):
                    m = 5 * c + g
                    par = (s + g) % 2
                    pe.wait_ge(proj_out, 5 * c + g + 41)
                    if not isinstance(m, int) or m >= 2:
                        if not (isinstance(m, int) and m < 2):
                            pe.wait_ge(kvt_out, m - 1)
                    if g < 4:
                        for i in range(4):
                            at = (4 * g + i) * P
                            mm = pe.transpose(ps[:, 5 + par, i * P:(i + 1) * P], B_VT[s][:, at:at + P], ident[:, :])
                    else:
                        mm = pe.transpose(ps[0:TS, 5 + par, 0:P], B_VT[s][:, SEQ:TOK], ident[:, :])
                    mm.then_inc(kvt_mm, 1)

            pe.wait_ge(misc_in, 64)
            for g in range(4):
                project(g, g % 2, g == 0)
                last_rows(g)
                if g:
                    mix_pool(g - 1)
            with pe.Fori(0, 2) as i:
                for s in range(2):
                    project(2 * i + s + 4, s)
            mix_pool(3)
            pe.wait_ge(wpool_out, 20)
            for c in range(2):
                project(8 + c, c)
                token_rows(c, c)
            with pe.Fori(1, 4) as i:
                for s in range(2):
                    project(2 * i + s + 8, s)
                    token_rows(2 * i + s, s)

            def scores(hp, u):
                b, kc = UNITS[u % NU]
                r = slice(HD * (u // NU), HD * (u // NU) + HD)
                for j in range(4):
                    z = 8 * NU * hp + 4 * u + j
                    w = (j + 1) * P if kc == b else BLK
                    qt = (4 * b + j) * P
                    if u:
                        pe.wait_ge(be_set, z - 3)
                    mm = pe.matmul(ps[:, j, 0:w], C_Q[r, qt:qt + P], C_K[r, BLK * kc:BLK * kc + w],
                                   start=True, stop=True)
                    if kc == b:
                        mm = pe.matmul(ps[:, j, w - P:w], ident_b[:, :], mask_b[:, :], start=False, stop=True,
                                       skip_group_check=True)
                    mm.then_inc(z_mm, 1)

            def turn_weights(hp, u, kt):
                b, kc = UNITS[u % NU]
                par = u % 2
                j0 = kt if kc == b else 0
                m = 8 * NU * hp + 4 * u + kt
                if kt == 0:
                    pe.wait_ge(prod_set, 8 * NU * hp + 4 * u + 4)
                done = at_act if kt % 2 == 0 else at_dve
                if kt >= 2:
                    pe.wait_ge(done, 4 * NU * hp + 2 * u + 1)
                elif u:
                    pe.wait_ge(done, 4 * NU * hp + 2 * u)
                for j in range(j0, 4):
                    mm = pe.transpose(ps[:, 4 + kt % 2, j * P:(j + 1) * P], C_A[:, par, j, kt * P:(kt + 1) * P], ident[:, :])
                mm.then_inc(at_mm, 1)

            def weigh(hp, u, kt):
                b, kc = UNITS[u % NU]
                e = u // NU
                r = slice(HD * e, HD * e + HD)
                j0 = kt * P if kc == b else 0
                done = at_act if kt % 2 == 0 else at_dve
                pe.wait_ge(done, 4 * NU * hp + 2 * u + kt // 2 + 1)
                if kc == b and kt == 0 and (b >= 2 or e):
                    pe.wait_ge(o_scaled, 8 * hp + 4 * e + b - 1)
                pe.matmul(ps[r, 6 + b % 2, j0:BLK], C_V[:, 4 * kc + kt, r], C_AT[kt][:, j0:BLK],
                          start=(kc == b and kt == 0), stop=(kc == 0 and kt == 3),
                          skip_group_check=True).then_inc(av_mm, 1)

            pe.wait_ge(kvt_out, 40)
            pe.wait_ge(npool_out, 4)
            with pe.Fori(0, NPAIR) as hp:
                pe.wait_ge(head_in[0], 48 * hp + 48)
                scores(hp, 0)
                for u in range(2 * NU):
                    if u == NU - 1:
                        pe.wait_ge(head_in[1], 48 * hp + 48)
                    if u < 2 * NU - 1:
                        scores(hp, u + 1)
                    turn_weights(hp, u, 0)
                    turn_weights(hp, u, 1)
                    weigh(hp, u, 0)
                    turn_weights(hp, u, 2)
                    weigh(hp, u, 1)
                    turn_weights(hp, u, 3)
                    weigh(hp, u, 2)
                    weigh(hp, u, 3)
            pe.wait_ge(smp_in, 64)
            pe.wait_ge(at_dve, 8 * NU * NPAIR // 2)
            pe.wait_ge(at_act, 8 * NU * NPAIR // 2)
            for hp in range(NPAIR):
                if hp >= 2:
                    pe.wait_ge(ck_set, hp - 1)
                for i in range(4):
                    mm = pe.transpose(ps[:, 4 + hp % 2, i * P:(i + 1) * P], C_CK[:, i, hp * P:(hp + 1) * P], ident[:, :])
                mm.then_inc(ck_mm, 1)
            pe.wait_ge(ck_set, 4)
            pe.wait_ge(be_set, 8 * NU * NPAIR)
            for g in range(2):
                for i in range(4):
                    h = 4 * g + i
                    r = slice(HD * (h % 2), HD * (h % 2) + HD)
                    o = slice(TS * i, TS * i + TS)
                    pe.matmul(ps[o, 2 * g, 0:PAST], C_QS[r, h // 2, :], C_CKT[r, h // 2, :], start=True, stop=True)
                    pe.matmul(ps[o, 2 * g + 1, 0:TS], C_QS[r, h // 2, :], C_KS[r, h // 2, :], start=True, stop=False)
                    mm = pe.matmul(ps[o, 2 * g + 1, 0:TS], ident_b[0:TS, 0:TS], mask_b[0:TS, 0:TS],
                                   start=False, stop=True)
                mm.then_inc(sz_mm, 1)
            pe.wait_ge(o_scaled, 8 * NPAIR)
            for g in range(2):
                pe.wait_ge(sprod, g + 1)
                for i in range(4):
                    pe.transpose(ps[:, 4 + g, i * P:(i + 1) * P], C_SA[g][:, i * P:(i + 1) * P], ident[:, :])
                pe.transpose(ps[0:TS, 6 + g, 0:P], C_SA[g][:, PAST:PAST + TS], ident[:, :]).then_inc(sat_mm, 1)
            pe.wait_ge(sat_set, 4)
            pe.wait_ge(ssig, 8)
            cv = B_CV.rearrange("p (i c) -> p i c", c=512)
            for h in range(NH):
                g, i, hp = h // 4, h % 4, h // 2
                r = slice(HD * (h % 2), HD * (h % 2) + HD)
                for kt in range(5):
                    if kt < 4:
                        lhs, rhs = cv[:, kt, h * HD:(h + 1) * HD], C_SAT[g][:, kt * P + TS * i:kt * P + TS * (i + 1)]
                    else:
                        lhs, rhs = C_VN[0:TS, h * HD:(h + 1) * HD], C_SAT[g][0:TS, 512 + TS * i:512 + TS * (i + 1)]
                    mm = pe.matmul(ps[r, 0, hp * TS:(hp + 1) * TS], lhs, rhs, start=(kt == 0), stop=(kt == 4))
            mm.then_inc(so_mm, 1)

            pe.wait_ge(fin_set, 1)
            for b in range(2):
                for n in range(2):
                    pe.matmul(ps[:, 4 + 2 * b + n, :], B_SEL[0:2, b, :], D_G1ROW[0:2, 512 * n:512 * (n + 1)],
                              start=True, stop=True).then_inc(g1_mm, 1)
            pe.wait_ge(so_split, 1)
            pe.wait_ge(o_split, 8 * NPAIR)
            pe.wait_ge(wo_lo, KD)
            pe.wait_ge(wo_hi, KD)
            pe.wait_ge(g1_set, 4)

            def mix_out(t, s, first=False, rows=P):
                if not first:
                    pe.wait_ge(d_mo, t - 1)
                for n in range(2):
                    for k in range(KD):
                        for xh, wh in TERMS:
                            mm = pe.matmul(ps[0:rows, 2 * s + n, :], hidden_t[:, t, k, xh, 0:rows],
                                           D_WO[:, wh, k, 512 * n:512 * (n + 1)],
                                           start=(k == 0 and (xh, wh) == (0, 0)),
                                           stop=(k == KD - 1 and (xh, wh) == TERMS[-1]))
                mm.then_inc(d_mm, 1)

            mix_out(0, 0, True)
            mix_out(1, 1, True)
            mix_out(2, 0)
            turn(0, 0, D_XH, d_xhat, d_tr, 4, d_full, True)
            mix_out(3, 1)
            turn(1, 1, D_XH, d_xhat, d_tr, 4, d_full, True)
            with pe.Fori(2, 8) as i:
                for s in range(2):
                    mix_out(2 * i + s, s)
                    turn(2 * i + s - 2, s, D_XH, d_xhat, d_tr, 4, d_full)
            mix_out(16, 0, False, TS)
            turn(14, 0, D_XH, d_xhat, d_tr, 4, d_full)
            turn(15, 1, D_XH, d_xhat, d_tr, 4, d_full)
            turn(16, 0, D_XH, d_xhat, d_tr, 4, d_full, False, TS)

            pe.wait_ge(d_hi, NT + 1)
            pe.wait_ge(d_lo, NT + 1)

            def gate_up(n, m, s, nb, grp, first=False):
                pe.wait_ge(gu_hi, n + 1)
                pe.wait_ge(gu_lo, n + 1)
                for blk in range(nb):
                    if not first:
                        pe.wait_ge(hid_set, m + blk + 1 - nb)
                    for w in range(2):
                        if blk < 2:
                            out = bank(2 * blk + w, BLK, 0)
                        else:
                            out = ps[:, 4, w * TS:(w + 1) * TS]
                        for k in range(KD):
                            for wh, xh in TERMS:
                                mm = pe.matmul(out, E_GHL[s][:, wh, k, w, :], moving(k, xh, 2 * grp + blk),
                                               start=(k == 0 and (wh, xh) == (0, 0)),
                                               stop=(k == KD - 1 and (wh, xh) == TERMS[-1]))
                    mm.then_inc(gu_mm, 1)

            def down(m, n, s, nb, first=False):
                pe.wait_ge(wd_hi, n)
                pe.wait_ge(wd_lo, n)
                for blk in range(nb):
                    if not first:
                        pe.wait_ge(dn_out, m + blk + 1 - nb)
                    w = BLK if blk < 2 else TS
                    for j in range(NF):
                        for wh, xh in TERMS:
                            mm = pe.matmul(ps[:, (0, 1, 4)[blk], 0:w], E_DHL[s][:, wh, j, :],
                                           E_HID[:, j, xh, BLK * blk:BLK * blk + w],
                                           start=(j == 0 and (wh, xh) == (0, 0)),
                                           stop=(j == NF - 1 and (wh, xh) == TERMS[-1]))
                    mm.then_inc(dn_mm, 1)

            def turn_back(n, rows=P, first=False):
                if not first:
                    pe.wait_ge(e_res, n)
                src = hidden_t[:, n, :, :, :].bitcast(f32).rearrange("p k a t -> p (k a t)")
                for k in range(KD):
                    mm = pe.transpose(ps[0:rows, 5 + k // 4, (k % 4) * P:(k % 4 + 1) * P], src[:, k * P:k * P + rows],
                                      ident[:, :])
                mm.then_inc(e_tr, 1)

            for grp in range(2):
                nb = 2 + grp
                m0, n0, h0, d0 = 2 * NF * grp, NF * grp, 16 * grp, 16 * grp
                if grp == 1:
                    pe.wait_ge(dn_out, 16)
                for j in range(2):
                    gate_up(n0 + j, m0 + nb * j, j, nb, grp, j == 0)
                    if grp == 1:
                        turn_back(j, first=(j == 0))
                if grp == 0:
                    with pe.Fori(1, NF // 2) as i:
                        for s in range(2):
                            gate_up(n0 + 2 * i + s, m0 + nb * (2 * i + s), s, nb, grp)
                else:
                    for j in range(2, 8):
                        gate_up(n0 + j, m0 + nb * j, j % 2, nb, grp)
                        turn_back(j)
                    with pe.Fori(4, NF // 2) as i:
                        for s in range(2):
                            gate_up(n0 + 2 * i + s, m0 + nb * (2 * i + s), s, nb, grp)
                m1 = m0 + nb * NF
                pe.wait_ge(hid_set, m1)
                pe.wait_ge(hid_hi, m1)
                pe.wait_ge(hid_lo, m1)
                down(d0, h0 + 2, 0, nb, True)
                down(d0 + nb, h0 + 4, 1, nb)
                with pe.Fori(1, KD // 2) as i:
                    for s in range(2):
                        down(d0 + nb * (2 * i + s), h0 + 4 * i + 2 * s + 2, s, nb)
            pe.wait_ge(dn_out, 40)
            for n in range(8, NT + 1):
                turn_back(n, P if n < NT else TS)
    return nc


INPUTS = ["x_prompt", "x_sample", "cache_k", "cache_v", "state_pool", "c_prompt", "c_sample",
          "w_ada", "b_ada", "w_in", "w_pool", "pool_scale", "w_o", "ln1_g", "ln1_b",
          "w_gu", "w_down", "ln2_g", "ln2_b"]
OUTPUTS = [(1, SEQ, D), (1, TS, D), (1, 1, SEQ, NH, HD), (1, 1, SEQ, NH, HD), (1, 1, HIST, PW),
           (1, 1, TS, NH, HD), (1, 1, TS, NH, HD), (1, 1, HIST, PW)]


def kernel(**inputs):
    import numpy as np
    import concourse.bacc as bacc
    from concourse.bass_utils import run_bass_kernel_spmd

    nc = bacc.Bacc("TRN2", target_bir_lowering=False, num_devices=1)
    arrays, args = {}, []
    for name in INPUTS:
        a = np.ascontiguousarray(inputs[name])
        arrays[f"in_{name}"] = a
        args.append(nc.dram_tensor(f"in_{name}", a.shape, mybir.dt.from_np(a.dtype), kind="ExternalInput").ap())
    for i, shape in enumerate(OUTPUTS):
        args.append(nc.dram_tensor(f"out_{i}", shape, f32, kind="ExternalOutput").ap())
    encoder_step(nc, *args)
    r = run_bass_kernel_spmd(nc, [arrays], core_ids=[0])
    return tuple(r.results[0][f"out_{i}"] for i in range(len(OUTPUTS)))
```

```python
import concourse.bass as bass
from concourse import mybir
from contextlib import ExitStack

f32 = mybir.dt.float32
f16 = mybir.dt.float16
bf16 = mybir.dt.bfloat16
i32 = mybir.dt.int32
ALU = mybir.AluOpType
ACT = mybir.ActivationFunctionType
AX = mybir.AxisListType
RMAX = bass.bass_isa.ReduceOp.max

P = 128
D = 1024
KD = D // P
SEQ = 2048
NT = SEQ // P
TS = 32
TOK = SEQ + TS
PAST = 512
HIST = 15
PW = 512
SBW = 512
HD = 64
NH = SBW // HD
NPAIR = NH // 2
FF = 2816
NF = FF // P
BLK = 512
ALPHA = 2.0 ** 0.25
EPS = 1e-5
SCALE = HD ** -0.5
TOP = 14
FAR = -1.0e30
HW = P * KD * 2
SBCOLS = 1056
LN_ROOT = 32.0


def encoder_step(nc, x_prompt, x_sample, cache_k, cache_v, state_pool, c_prompt, c_sample,
                 w_ada, b_ada, w_in, w_pool, pool_scale, w_o, ln1_g, ln1_b,
                 w_gu, w_down, ln2_g, ln2_b,
                 y_prompt, y_sample, new_k_prompt, new_v_prompt, new_pool_prompt,
                 new_k_sample, new_v_sample, new_pool_sample):
    ctx = ExitStack()
    with ctx:
        def sb(name, shape, dt):
            return ctx.enter_context(nc.sbuf_tensor(name, shape, dt))

        def sem(name):
            return ctx.enter_context(nc.semaphore(name))

        q_s_dram = nc.dram_tensor("q_s_dram", (NPAIR, P, TS), f32).ap()
        k_s_dram = nc.dram_tensor("k_s_dram", (NPAIR, P, TS), f32).ap()
        q_hl_dram = nc.dram_tensor("q_hl_dram", (NPAIR, 2, P, SEQ), f16).ap()
        k_hl_dram = nc.dram_tensor("k_hl_dram", (NPAIR, 2, P, SEQ), f16).ap()
        pool_dram = nc.dram_tensor("pool_dram", (4, P, TOK), f32).ap()
        x1_dram = nc.dram_tensor("x1_dram", (TOK, D), f32).ap()

        ident = sb("ident", [P, P], f32)
        ident_b = sb("ident_b", [P, P], bf16)
        mask_b = sb("mask_b", [P, P], bf16)
        ln2_rows = sb("ln2_rows", [P, 2, D], f32)
        mod_t = sb("mod_t", [P, 6, KD, 2], f32)
        col = sb("col", [P, 88], f32)
        small = sb("small", [P, 112], f32)
        hidden_t = sb("hidden_t", [P, NT + 1, KD, 2, P], f16)
        WORK = 33000
        work = sb("work", [P, WORK], f32)
        ps = ctx.enter_context(nc.psum_tensor("ps", [P, 8, 512], f32))

        def w32(at, n):
            assert at + n <= WORK, (at, n)
            return work[:, at:at + n]

        def w16(at, n):
            assert at + n // 2 <= WORK, (at, n)
            return work[:, at:at + n // 2].bitcast(f16)

        C_NEGHALF, C_SH, C_FH, C_SH2, C_FH2 = 0, 1, 2, 3, 4
        C_SGU, C_SWD, C_SWO, C_SMIX = 5, 6, 7, 8
        C_FGU, C_FWD, C_FWO, C_FMIX, C_SHID, C_FHID = 9, 10, 11, 12, 13, 14
        C_F1, C_F2, C_FWOMIX, C_FDOWN = 15, 16, 17, 18
        C_W = 20
        C_EPS = 19
        C_PSCALE = 24
        C_BOUND = 28
        C_POOLMAX = 36
        C_VMAX = 40
        C_TS, C_TF = 64, 72
        C_ZNOW = 61
        C_SPARE = 63
        C_Z = 80
        C_INV = 46

        def c1(i, n=1):
            return col[:, i:i + n]

        A_X = [w32(0, 1024), w32(1024, 1024)]
        A_XH = [w32(2048, 1024), w32(3072, 1024)]
        A_HF = [w32(4096, 1024), w32(5120, 1024)]
        A_WADA = w32(6144, 16384).rearrange("p (s k n) -> p s k n", s=4, k=KD)
        A_BROW = w32(22528, 128)
        A_MROW = w32(22656, 2048)
        A_CROW = w32(26624, 128)
        CT = small[:, 96:112].rearrange("p (b k) -> p b k", b=2)
        A_CSIG = w32(26768, 16)
        A_HISTROW = w32(26784, 512)
        A_STAT = [w32(27296, 16), w32(27312, 16)]
        A_RS = [w32(27328, 4), w32(27332, 4)]
        B_RAW = [w32(6144, 1024), w32(7168, 1024)]
        B_HL = [w16(8192, 2048), w16(9216, 2048)]
        UW = 2112
        B_U = w32(10240, UW)
        B_S = [w32(12352, UW), w32(14464, UW)]
        B_THL = [w16(23360 + 2048 * s, 4096).rearrange("p (h t) -> p h t", h=2) for s in range(2)]
        B_VT = [w32(12352, TOK), w32(14464, TOK)]
        B_STG = [w32(16576, 512), w32(17088, 512)]
        B_WPOOL = w32(17600, 512)
        B_NPOOL = w32(18112, 1024)
        B_QT = [w32(19200, TOK), w32(21280, TOK)]
        B_CV = w32(28700, 2048)
        HIST_T = w32(30748, 60)
        C_Q = [w16(1024 * e, 2048) for e in range(2)]
        C_K = [w16(at, 4096).rearrange("p (h t) -> p h t", h=2) for at in (2048, 24384)]
        C_VHL = w16(4096, 4096).rearrange("p (e i c) -> p e i c", e=2, i=NT)
        PB = 516
        C_PR = w32(6144, 8 * PB)
        C_A = w32(10272, 4096).rearrange("p (s j n) -> p s j n", s=2, j=4)
        C_AT = [w16(14368 + 512 * i, 1024).rearrange("p (h n) -> p h n", h=2) for i in range(4)]
        C_ST = [w32(16416, 512), w32(16928, 512)]
        C_PIECE = [w32(17440, TOK), w32(30810, 2048)]
        C_CK = w32(19520, 2048).rearrange("p (i c) -> p i c", c=512)
        C_CKT = w32(21568, 2048).rearrange("p (h t) -> p h t", h=4)
        C_VRAW = [w32(21568 + D * e, D).rearrange("p (i c) -> p i c", c=HD) for e in range(2)]
        C_QS = w32(23616, 128).rearrange("p (h t) -> p h t", h=4)
        C_KS = w32(23744, 128).rearrange("p (h t) -> p h t", h=4)
        C_VN = w32(23872, 512)
        C_SP = [w32(24384, 548), w32(24932, 548)]
        C_SA = [w32(25480, 544), w32(26024, 544)]
        C_SAT = [w32(26568, 640), w32(27208, 640)]
        C_SST = w32(27848, 128)
        C_OLOW = w32(26568, 512)
        MOD_ROW = w32(27976, 256)
        D_WO = w16(0, 16384).rearrange("p (h k n) -> p h k n", h=2, k=KD)
        D_X = [w32(8192, 1024), w32(9216, 1024)]
        D_R = [w32(10240, 1024), w32(11264, 1024)]
        D_X1 = [w32(12288, 1024), w32(13312, 1024)]
        D_XH = [w32(14336, 1024), w32(15360, 1024)]
        D_RAW = D_X1 + D_XH
        D_HF = [w32(16384, 1024), w32(17408, 1024)]
        D_G1 = w32(18432, 2048).rearrange("p (b n) -> p b n", b=2)
        D_LN1 = w32(20480, 2048).rearrange("p (b n) -> p b n", b=2)
        D_STAT = [w32(22528, 16), w32(22544, 16)]
        D_ONES = w32(22560, P)
        D_REP = w32(16384, 2048).rearrange("p (b k m) -> p b k m", b=2, k=KD)
        E_HID = w16(0, NF * 2 * SBCOLS).rearrange("p (j h t) -> p j h t", j=NF, h=2)
        E0 = NF * SBCOLS
        E_GRAW = w32(E0, 2048).rearrange("p (k w n) -> p k w n", k=KD, w=2)
        E_GHL = [w16(E0 + 2048 + 3072 * s, 4096).rearrange("p (h k w n) -> p h k w n", h=2, k=KD, w=2)
                 for s in range(2)]
        E_DRAW = w32(E0, 1408).rearrange("p (j n) -> p j n", n=P)
        E_DHL = [w16(E0 + 1408 + 2816 * s, 5632).rearrange("p (h j n) -> p h j n", h=2, j=NF)
                 for s in range(2)]
        E1 = E0 + 7168
        E_SIG = w32(E1, 512)
        E_T = w32(E1 + 512, 512)
        E_H = w32(E1 + 1024, 512)
        E_X1 = [w32(E1 + 1536, 1024), w32(E1, 1024)]
        E_STAT = [w32(32980, 16), w32(E1 + 1024, 16)]

        consts_set = sem("consts_set")
        crow_in, brow_in, hist_in = sem("crow_in"), sem("brow_in"), sem("hist_in")
        wada_in = [sem(f"wada_in{s}") for s in range(4)]
        x_in = [sem("x_in0"), sem("x_in1")]
        misc_in = sem("misc_in")
        ct_mm, csig_set, ct_set = sem("ct_mm"), sem("csig_set"), sem("ct_set")
        ada_mm, ada_row, mod_turned, mod_max, mod_ar, mod_set = sem("ada_mm"), sem("ada_row"), sem("mod_turned"), sem("mod_max"), sem("mod_ar"), sem("mod_set")
        dve = sem("dve_steps")
        pool_steps = sem("pool_steps")
        a_aggr, a_rstd, a_xhat = sem("a_aggr"), sem("a_rstd"), sem("a_xhat")
        a_tr, a_full, a_hi, a_lo = sem("a_tr"), sem("a_full"), sem("a_hi"), sem("a_lo")
        hist_mm, hist_set = sem("hist_mm"), sem("hist_set")
        w_in_raw = [sem("w_in_raw0"), sem("w_in_raw1")]
        w_mx, w_ar, w_s, w_hi, w_lo = sem("w_mx"), sem("w_ar"), sem("w_s"), sem("w_hi"), sem("w_lo")
        proj_mm, proj_out = sem("proj_mm"), sem("proj_out")
        pooled_set, wpool_mm, wpool_out, rmax_set = sem("pooled_set"), sem("wpool_mm"), sem("wpool_out"), sem("rmax_set")
        pool_stored = sem("pool_stored")
        npool_mm, npool_out = sem("npool_mm"), sem("npool_out")
        q_stored = [sem("q_stored0"), sem("q_stored1")]
        k_stored = [sem("k_stored0"), sem("k_stored1")]
        t_hi, t_lo = sem("t_hi"), sem("t_lo")
        kvt_mm, kvt_out = sem("kvt_mm"), sem("kvt_out")
        kv_stored = [sem("kv_stored0"), sem("kv_stored1")]
        vmax_set, mix_max, mix_ar, mix_set = sem("vmax_set"), sem("mix_max"), sem("mix_ar"), sem("mix_set")
        cv_in = sem("cv_in")
        fin_max, fin_ar, fin_set = sem("fin_max"), sem("fin_ar"), sem("fin_set")
        out_small = sem("out_small")
        head_in = [sem("head_in0"), sem("head_in1")]
        v_in, v_hi, v_lo, o_low = [sem("v_in0"), sem("v_in1")], sem("v_hi"), sem("v_lo"), sem("o_low")
        z_now = sem("z_now")
        piece_in = [sem("piece_in0"), sem("piece_in1")]
        piece_free = sem("piece_free")
        mod_new = sem("mod_new")
        z_mm, sg_set, be_set, scan_set, prod_set = (sem("z_mm"), sem("sg_set"), sem("be_set"),
                                                    sem("scan_set"), sem("prod_set"))
        at_mm, at_act, at_dve, av_mm = sem("at_mm"), sem("at_act"), sem("at_dve"), sem("av_mm")
        o_scaled, o_split = sem("o_scaled"), sem("o_split")
        smp_in = sem("smp_in")
        ck_mm, ck_set, sz_mm, ssig, sprod, sat_mm, sat_set, so_mm, so_split = (
            sem("ck_mm"), sem("ck_set"), sem("sz_mm"), sem("ssig"), sem("sprod"), sem("sat_mm"),
            sem("sat_set"), sem("so_mm"), sem("so_split"))
        g1_rep, g1_mm, g1_set = sem("g1_rep"), sem("g1_mm"), sem("g1_set")
        wo_raw = [sem(f"wo_raw{s}") for s in range(4)]
        wo_hi, wo_lo = sem("wo_hi"), sem("wo_lo")
        dx_in = [sem("dx_in0"), sem("dx_in1")]
        ln1_in = sem("ln1_in")
        d_mm, d_mo, d_res, d_aggr1, d_rstd1 = sem("d_mm"), sem("d_mo"), sem("d_res"), sem("d_aggr1"), sem("d_rstd1")
        d_x1, d_aggr2, d_rstd2, d_xhat = sem("d_x1"), sem("d_aggr2"), sem("d_rstd2"), sem("d_xhat")
        x1_stored = [sem("x1_stored0"), sem("x1_stored1")]
        d_tr, d_full, d_hi, d_lo = sem("d_tr"), sem("d_full"), sem("d_hi"), sem("d_lo")
        gu_raw, gu_hi, gu_lo = sem("gu_raw"), sem("gu_hi"), sem("gu_lo")
        gu_mm, sig_set, hid_set, hid_hi, hid_lo = sem("gu_mm"), sem("sig_set"), sem("hid_set"), sem("hid_hi"), sem("hid_lo")
        wd_raw, wd_hi, wd_lo = sem("wd_raw"), sem("wd_hi"), sem("wd_lo")
        dn_mm, dn_out = sem("dn_mm"), sem("dn_out")
        e_x1, y_stored = [sem("e_x1_0"), sem("e_x1_1")], [sem("y_stored0"), sem("y_stored1")]
        e_tr, e_res, e_aggr, e_rstd, e_y = (sem("e_tr"), sem("e_res"), sem("e_aggr"), sem("e_rstd"),
                                            sem("e_y"))

        class Steps:

            def __init__(self, eng, sem_):
                self.eng, self.sem, self.n, self.reg, self.lo, self.per = eng, sem_, 0, None, 0, 0

            def done(self, ins):
                ins.then_inc(self.sem, 1)
                self.n += 1

            def wait(self):
                if self.reg is None:
                    self.eng.wait_ge(self.sem, self.n)
                else:
                    self.eng.wait_ge(self.sem, (self.reg - self.lo) * self.per + self.n)

            def enter(self, reg, lo, per):
                self.reg, self.lo, self.per, self.entry = reg, lo, per, self.n

            def leave(self, count):
                assert self.n - self.entry == self.per, (self.n - self.entry, self.per)
                self.n = self.entry + self.per * count
                self.reg = None

        BLKS = [(0, BLK), (1, BLK), (2, BLK), (3, BLK), (4, TS)]

        def moving(k, hl, blk):
            if blk < 4:
                return hidden_t[:, 4 * blk:4 * blk + 4, k, hl, :]
            return hidden_t[:, NT, k, hl, 0:TS]

        def bank(b, n, blk):
            return ps[:, b, 0:n].rearrange("p (a t) -> p a t", t=P) if blk < 4 else ps[:, b, 0:n]

        TERMS = [(0, 0), (0, 1), (1, 0)]
        PRW = C_PR.rearrange("p (j s n) -> p j s n", j=4, s=2)
        UNITS = [(b, kc) for b in range(4) for kc in range(b, -1, -1)]
        NU = len(UNITS)
        PASSES = [(0, (0, 1), (0, 1), 0), (1, (0, 2), (0, 4), 16), (1, (1,), (1, 2), 32)]
        LN2_TILES = [*range(12), NT, *range(12, NT)]

        def ln2_uses(n):
            return n + 1 if n < 8 else 8 + (n - 8) // 2 + 1 if n % 2 == 0 else (n - 9) // 2 + 1
        xp_t = x_prompt.rearrange("b (i p) d -> (b i) p d", p=P)
        x1_t = x1_dram[0:SEQ, :].rearrange("(i p) d -> i p d", p=P)
        yp_t = y_prompt.rearrange("b (i p) d -> (b i) p d", p=P)
        w_in_c = w_in[0].rearrange("(k p) (c n) -> c p k n", p=P, n=P)
        w_gu_c = w_gu[0].rearrange("(k p) (w j n) -> j w p k n", p=P, w=2, n=P)
        w_dn_c = w_down[0].rearrange("(j p) (c n) -> c p j n", p=P, n=P)
        nk_p = new_k_prompt[0, 0].rearrange("(i p) h d -> i p (h d)", p=P)
        nv_p = new_v_prompt[0, 0].rearrange("(i p) h d -> i p (h d)", p=P)
        nk_s = new_k_sample[0, 0].rearrange("t h d -> t (h d)")
        nv_s = new_v_sample[0, 0].rearrange("t h d -> t (h d)")
        PIECES = "agmggmggggmgdddmdo"
        NPIECE = len(PIECES)
        PIECE_N = {"g": 1408, "d": 1408, "o": 2048}
        flat_of = {kind: w[0].rearrange("a b -> (a b)").rearrange("(p n) -> p n", p=P)
                   for kind, w in (("g", w_gu), ("d", w_down), ("o", w_o))}
        MAX_OF = [i for i, kind in enumerate(PIECES) if kind in "gdo"]
        NEW_MAX, ALL_MAX = small[:, 16:16 + len(MAX_OF)], small[:, 66:66 + len(MAX_OF)]
        w_ada_k = w_ada[0].rearrange("(k p) n -> p k n", p=P)

        def place(i):
            return PIECES[:i].count(PIECES[i])

        block = ctx.enter_context(nc.Block())

        @block.sync
        def _(sp):
            sp.dma_start(A_CROW[0:KD, :], c_prompt.rearrange("b (k p) -> (b k) p", p=P)).then_inc(crow_in, 16)
            sp.dma_start(A_CROW[KD:2 * KD, :], c_sample.rearrange("b (k p) -> (b k) p", p=P)).then_inc(crow_in, 16)
            sp.dma_start(A_BROW[0:48, :], b_ada[0:1, :].rearrange("o (r p) -> (o r) p", p=P)).then_inc(brow_in, 16)

            def load_ada(s):
                sp.dma_start(A_WADA[:, s, :, :], w_ada_k[:, :, 512 * s:512 * (s + 1)]).then_inc(wada_in[s], 16)

            def load_x(t, s):
                sp.dma_start(A_X[s], xp_t[t]).then_inc(x_in[s], 16)

            def load_w(c, s):
                sp.dma_start(B_RAW[s].rearrange("p (k n) -> p k n", k=KD), w_in_c[c]).then_inc(w_in_raw[s], 16)

            load_ada(0)
            load_ada(1)
            load_x(0, 0)
            load_x(1, 1)
            load_ada(2)
            load_ada(3)
            for s in range(2):
                sp.wait_ge(a_xhat, s + 1)
                load_x(2 + s, s)
            sp.wait_ge(ada_mm, 1)
            load_w(0, 0)
            load_w(1, 1)
            sp.dma_start(A_HISTROW[0:HIST, :], state_pool[0, 0]).then_inc(hist_in, 16)
            sp.dma_start(ln2_rows[:, 0, :], ln2_g[0:1, :].partition_broadcast(P)).then_inc(misc_in, 16)
            sp.dma_start(ln2_rows[:, 1, :], ln2_b[0:1, :].partition_broadcast(P)).then_inc(misc_in, 16)
            sp.dma_start(col[:, C_PSCALE:C_PSCALE + 4],
                         pool_scale[0].rearrange("(g p) -> p g", p=P),
                         allow_slow_non_contiguous=True).then_inc(misc_in, 16)
            sp.wait_ge(ada_mm, 4)
            sp.dma_start(B_WPOOL.rearrange("p (g n) -> p g n", g=4),
                         w_pool[0].rearrange("g p n -> p g n")).then_inc(misc_in, 16)
            with sp.Fori(1, 7) as i:
                for s in range(2):
                    sp.wait_ge(a_xhat, 2 * i + s + 1)
                    load_x(2 * i + s + 2, s)
            sp.wait_ge(a_xhat, 15)
            sp.dma_start(A_X[0][0:TS, :], x_sample[0]).then_inc(x_in[0], 16)
            sp.dma_start(B_CV.rearrange("p (i c) -> p i c", c=512),
                         cache_v[0, 0].rearrange("(i p) h d -> p i (h d)", p=P)).then_inc(cv_in, 16)

            def next_w(c, s):
                sp.wait_ge(w_lo, c + 1)
                load_w(c + 2, s)

            def store_pool(g):
                sp.wait_ge(wpool_out, 5 * (g + 1))
                sp.dma_start(pool_dram[g], B_S[g % 2][:, 0:TOK]).then_inc(pool_stored, 16)

            for g in range(4):
                next_w(g, g % 2)
                if g:
                    store_pool(g - 1)

            with sp.Fori(0, 2) as i:
                for u in range(2):
                    next_w(4 + 2 * i + u, u)
                    sp.wait_ge(proj_out, 5 * (2 * i + u) + 25)
                    sp.dma_start(q_s_dram[2 * i + u], B_QT[u][:, SEQ:TOK]).then_inc(q_stored[u], 16)
                    sp.wait_ge(t_lo, 2 * i + u + 1)
                    sp.dma_start(q_hl_dram[2 * i + u].rearrange("h p t -> p h t"), B_THL[u]).then_inc(q_stored[u], 16)
            store_pool(3)
            for s in range(2):
                sp.wait_ge(q_stored[s], 64)

            def load_qk(hp, e):
                r = slice(HD * e, HD * e + HD)
                for half in range(2):
                    rows = slice(HD * half, HD * half + HD)
                    sp.dma_start(C_Q[e][rows, :], q_hl_dram[hp, half, r, :]).then_inc(head_in[e], 16)
                    sp.dma_start(C_K[e][rows, :, :], k_hl_dram[hp, :, r, :].rearrange("h p t -> p h t")
                                 ).then_inc(head_in[e], 16)

            def load_v(hp, e):
                sp.dma_start(C_VRAW[e], nv_p[:, :, bass.ds(hp * P + HD * e, HD)].rearrange("i p c -> p i c")
                             ).then_inc(v_in[e], 16)

            def store_rows(c, u, prompt, sample):
                for g in range(5):
                    sp.wait_ge(kvt_out, 5 * c + g + 1)
                    slot = (u + g) % 2
                    ch = (c % 4 if isinstance(c, int) else c)
                    if g < 4:
                        dst = prompt[4 * g:4 * g + 4, :, bass.ds(ch * P, P)].rearrange("i p c -> p i c")
                        sp.dma_start(dst, B_STG[slot].rearrange("p (i c) -> p i c", c=P)).then_inc(kv_stored[slot], 16)
                    else:
                        sp.dma_start(sample[:, bass.ds(ch * P, P)], B_STG[slot][0:TS, 0:P]).then_inc(kv_stored[slot], 16)

            with sp.Fori(0, 2) as i:
                for u in range(2):
                    c = 2 * i + u
                    next_w(8 + c, u)
                    sp.wait_ge(proj_out, 5 * c + 45)
                    sp.dma_start(k_s_dram[c], B_VT[u][:, SEQ:TOK]).then_inc(k_stored[u], 16)
                    sp.wait_ge(t_lo, c + 5)
                    sp.dma_start(k_hl_dram[c].rearrange("h p t -> p h t"), B_THL[u]).then_inc(k_stored[u], 16)
                    store_rows(c, u, nk_p, nk_s)
            for c in range(4, 8):
                if c < 6:
                    next_w(8 + c, c % 2)
                if c == 5:
                    for s in range(2):
                        sp.wait_ge(k_stored[s], 64)
                    for e in range(2):
                        load_qk(0, e)
                store_rows(c, c % 2, nv_p, nv_s)
                if c == 6:
                    for s in range(2):
                        sp.wait_ge(kv_stored[s], 240)
                    for e in range(2):
                        load_v(0, e)
            sp.wait_ge(npool_out, 4)
            sp.dma_start(new_pool_prompt[0, 0], B_NPOOL[0:HIST, 0:PW]).then_inc(out_small, 16)
            sp.dma_start(new_pool_sample[0, 0], B_NPOOL[0:HIST, PW:2 * PW]).then_inc(out_small, 16)
            for s in range(2):
                sp.wait_ge(kv_stored[s], 320)

            def load_piece(hp, i):
                s = i % 2
                kind = PIECES[i]
                sp.wait_ge(piece_free, NPIECE * hp + i + 1)
                if kind == "a":
                    ins = sp.dma_start(C_PIECE[0], pool_dram[hp])
                elif kind == "m":
                    ins = sp.dma_start(C_PIECE[s][:, 0:2048].rearrange("p (k n) -> p k n", k=KD),
                                       w_ada_k[:, :, bass.ds(hp * D + 2 * D + 256 * place(i), 256)])
                else:
                    n = PIECE_N[kind]
                    ins = sp.dma_start(C_PIECE[s][:, 0:n],
                                       flat_of[kind][:, bass.ds(hp * (PIECES.count(kind) * n) + place(i) * n, n)])
                ins.then_inc(piece_in[s], 16)

            sp.wait_ge(pool_stored, 64)
            sp.dma_start(C_CK, cache_k[0, 0].rearrange("(i p) h d -> p i (h d)", p=P)).then_inc(smp_in, 16)
            sp.dma_start(C_QS, q_s_dram.rearrange("h p t -> p h t")).then_inc(smp_in, 16)
            sp.dma_start(C_KS, k_s_dram.rearrange("h p t -> p h t")).then_inc(smp_in, 16)
            sp.dma_start(C_VN[0:TS, :], nv_s).then_inc(smp_in, 16)
            def load_head(hp, e):
                sp.wait_ge(av_mm, (hp - 1) * (8 * NU) + 4 * NU * (e + 1))
                sp.wait_ge(v_lo, 2 * (hp - 1) + e + 1)
                load_qk(hp, e)
                load_v(hp, e)

            def load_pair(hp, behind, ahead):
                for i in range(NPIECE):
                    load_piece(hp, i)
                    if i == 3 and behind:
                        load_head(hp, 1)
                    if i == 13 and ahead:
                        load_head(hp + 1, 0)

            load_pair(0, False, True)
            with sp.Fori(1, NPAIR - 1) as hp:
                load_pair(hp, True, True)
            load_pair(NPAIR - 1, True, False)

            sp.wait_ge(av_mm, 8 * NU * NPAIR)
            w_o_k = w_o[0].rearrange("(k p) n -> k p n", p=P)
            for k in range(KD):
                if k >= 4:
                    sp.wait_ge(wo_lo, k - 3)
                sp.dma_start(D_RAW[k % 4], w_o_k[k]).then_inc(wo_raw[k % 4], 16)

            sp.wait_ge(so_split, 1)
            sp.dma_start(D_LN1[:, 0, :], ln1_g[0:1, :].partition_broadcast(P)).then_inc(ln1_in, 16)
            sp.dma_start(D_LN1[:, 1, :], ln1_b[0:1, :].partition_broadcast(P)).then_inc(ln1_in, 16)

            def load_dx(t, s):
                sp.dma_start(D_X[s], xp_t[t]).then_inc(dx_in[s], 16)

            load_dx(0, 0)
            load_dx(1, 1)

            def load_gu(c):
                for w in range(2):
                    sp.dma_start(E_GRAW[:, :, w, :], w_gu_c[c, w]).then_inc(gu_raw, 16)

            load_gu(0)

            def step_d(t, s):
                sp.wait_ge(d_res, t + 1)
                load_dx(t + 2, s)
                sp.wait_ge(d_x1, t + 1)
                sp.dma_start(x1_t[t], D_X1[s]).then_inc(x1_stored[s], 16)

            with sp.Fori(0, 7) as i:
                for s in range(2):
                    step_d(2 * i + s, s)
            sp.wait_ge(d_res, 15)
            sp.dma_start(D_X[0][0:TS, :], x_sample[0]).then_inc(dx_in[0], 16)
            for t in (14, 15):
                sp.wait_ge(d_x1, t + 1)
                sp.dma_start(x1_t[t], D_X1[t % 2]).then_inc(x1_stored[t % 2], 16)
            sp.wait_ge(d_x1, 17)
            sp.dma_start(x1_dram[SEQ:TOK, :], D_X1[0][0:TS, :]).then_inc(x1_stored[0], 16)
            sp.wait_ge(x1_stored[0], 9 * 16)
            sp.wait_ge(x1_stored[1], 8 * 16)

            def load_dn(c, half):
                sp.dma_start(E_DRAW, w_dn_c[c][:, 11 * half:11 * half + 11, :]).then_inc(wd_raw, 16)

            def x1_in(n, s, tile):
                rows = x1_dram[SEQ:TOK, :] if isinstance(tile, int) and tile == NT else x1_t[tile]
                dst = E_X1[s][0:TS, :] if isinstance(tile, int) and tile == NT else E_X1[s]
                sp.dma_start(dst, rows).then_inc(e_x1[s], 16)

            def y_out(n, s, tile):
                sp.wait_ge(e_y, n + 1)
                if isinstance(tile, int) and tile == NT:
                    sp.dma_start(y_sample[0], E_X1[s][0:TS, :]).then_inc(y_stored[s], 16)
                else:
                    sp.dma_start(yp_t[tile], E_X1[s]).then_inc(y_stored[s], 16)

            with sp.Fori(1, NF) as c:
                sp.wait_ge(gu_lo, c)
                load_gu(c)
            sp.wait_ge(gu_lo, NF)
            load_dn(0, 0)
            sp.wait_ge(wd_lo, 1)
            load_dn(0, 1)
            with sp.Fori(1, KD) as c:
                for half in range(2):
                    sp.wait_ge(wd_lo, 2 * c + half)
                    load_dn(c, half)
            sp.wait_ge(wd_lo, 16)
            sp.wait_ge(dn_mm, 14)
            load_gu(0)
            sp.wait_ge(gu_lo, NF + 1)
            load_gu(1)
            x1_in(0, 0, 0)
            y_out(0, 0, 0)
            with sp.Fori(2, 9) as c:
                sp.wait_ge(gu_lo, c + NF)
                load_gu(c)
                sp.wait_ge(y_stored[0], 16 * (c - 1))
                x1_in(c - 1, 0, c - 1)
                y_out(c - 1, 0, c - 1)
            with sp.Fori(9, NF) as c:
                sp.wait_ge(gu_lo, c + NF)
                load_gu(c)
            sp.wait_ge(gu_lo, 2 * NF)
            load_dn(0, 0)
            sp.wait_ge(wd_lo, 17)
            load_dn(0, 1)
            with sp.Fori(1, KD) as c:
                for half in range(2):
                    sp.wait_ge(wd_lo, 2 * c + half + 16)
                    load_dn(c, half)
            sp.wait_ge(hid_lo, 5 * NF)
            for c in range(KD):
                n = 8 + c
                sp.wait_ge(wd_lo, 2 * c + 32)
                load_dn(c, 0)
                if 10 <= n <= 14:
                    y_out(n - 2, n % 2, LN2_TILES[n - 2])
                    sp.wait_ge(y_stored[n % 2], 16 * (ln2_uses(n) - 1))
                elif n == 8:
                    sp.wait_ge(y_stored[0], 16 * 8)
                sp.wait_ge(wd_lo, 2 * c + 33)
                load_dn(c, 1)
                if n <= 14:
                    x1_in(n, n % 2, LN2_TILES[n])
            for n in range(13, NT + 1):
                y_out(n, n % 2, LN2_TILES[n])
                if n <= NT - 2:
                    sp.wait_ge(y_stored[n % 2], 16 * ln2_uses(n))
                    x1_in(n + 2, n % 2, LN2_TILES[n + 2])
            for s in range(2):
                sp.wait_ge(y_stored[s], 16 * ln2_uses(16 - s))

        @block.gpsimd
        def _(pool):
            own = Steps(pool, pool_steps)
            own.done(pool.memset(ident[:, :], 1.0))
            own.done(pool.memset(mask_b[:, :], FAR))
            own.wait()
            own.done(pool.affine_select(out=ident[:, :], in_=ident[:, :], compare_op=ALU.is_equal, fill=0.0,
                                        base=0, pattern=[[-1, P]], channel_multiplier=1))
            own.done(pool.affine_select(out=mask_b[:, :], in_=mask_b[:, :], compare_op=ALU.is_ge, fill=0.0,
                                        base=0, pattern=[[1, P]], channel_multiplier=-1))
            own.wait()
            own.done(pool.tensor_copy(ident_b[:, :], ident[:, :]))
            for t in range(HIST):
                own.done(pool.memset(c1(C_INV + t), 1.0 / (t + 1)))
            own.done(pool.memset(c1(C_NEGHALF), -0.5))
            own.done(pool.memset(c1(C_EPS), EPS))
            own.wait()
            pool.memset(ALL_MAX, 0.0).then_inc(consts_set, 1)

            def rstd(stat):
                own.done(pool.tensor_tensor(stat[:, 14:15], stat[:, 13:14], c1(C_EPS), ALU.add))
                own.wait()
                return pool.tensor_tensor(stat[:, 15:16], stat[:, 14:15], c1(C_NEGHALF), ALU.pow)

            def all_max(dst, src):
                return pool.partition_all_reduce(dst, src, P, RMAX)

            def rstd_a(t, s):
                pool.wait_ge(a_aggr, t + 1)
                rstd(A_STAT[s]).then_inc(a_rstd, 1)

            def lo_a(t, s, rows=P):
                pool.wait_ge(a_hi, t + 1)
                pool.tensor_tensor(hidden_t[:, t, :, 1, 0:rows], A_HF[s].rearrange("p (k t) -> p k t", k=KD)[:, :, 0:rows],
                                   hidden_t[:, t, :, 0, 0:rows], ALU.subtract).then_inc(a_lo, 1)

            rstd_a(0, 0)
            rstd_a(1, 1)
            pool.wait_ge(mod_max, 1)
            all_max(small[:, 2:4], small[:, 0:2]).then_inc(mod_ar, 1)
            with pool.Fori(0, 7) as i:
                own.enter(i, 0, 2)
                for s in range(2):
                    rstd_a(2 * i + s + 2, s)
                    lo_a(2 * i + s, s)
            own.leave(7)
            rstd_a(16, 0)
            pool.wait_ge(w_mx, 1)
            all_max(small[:, 8:9], small[:, 6:7]).then_inc(w_ar, 1)
            lo_a(14, 0)
            lo_a(15, 1)
            lo_a(16, 0, TS)

            for c in range(1, 16):
                s = c % 2
                pool.wait_ge(w_mx, c + 1)
                all_max(small[:, 8 + s:9 + s], small[:, 6 + s:7 + s]).then_inc(w_ar, 1)
            pool.wait_ge(mix_max, 1)
            all_max(small[:, 47:48], small[:, 43:44]).then_inc(mix_ar, 1)

            with pool.Fori(0, NPAIR) as hp:
                for u in range(2 * NU):
                    b, kc = UNITS[u % NU]
                    par = u % 2
                    for j in range(4):
                        w = (j + 1) * P if kc == b else BLK
                        z = 8 * NU * hp + 4 * u + j
                        pool.wait_ge(scan_set, z + 1)
                        pool.wait_ge(be_set, z + 1)
                        pool.tensor_tensor(C_A[:, par, j, 0:w], C_A[:, par, j, 0:w],
                                           PRW[:, j, par, 1:w + 1], ALU.mult).then_inc(prod_set, 1)

            pool.wait_ge(fin_max, 1)
            all_max(small[:, 91:96], small[:, 86:91]).then_inc(fin_ar, 1)

            def rstd_d(ready, done, n, s):
                pool.wait_ge(ready, n)
                rstd(D_STAT[s]).then_inc(done, 1)

            def lo_d(t, s, rows=P):
                pool.wait_ge(d_hi, t + 1)
                pool.tensor_tensor(hidden_t[:, t, :, 1, 0:rows], D_HF[s].rearrange("p (k t) -> p k t", k=KD)[:, :, 0:rows],
                                   hidden_t[:, t, :, 0, 0:rows], ALU.subtract).then_inc(d_lo, 1)

            rstd_d(d_aggr1, d_rstd1, 1, 0)
            rstd_d(d_aggr2, d_rstd2, 1, 0)

            def two_d(i):
                for s in range(2):
                    t = 2 * i + s
                    rstd_d(d_aggr1, d_rstd1, t + 2, (s + 1) % 2)
                    rstd_d(d_aggr2, d_rstd2, t + 2, (s + 1) % 2)
                    lo_d(t, s)

            with pool.Fori(0, 8) as i:
                own.enter(i, 0, 4)
                two_d(i)
            own.leave(8)
            lo_d(16, 0, TS)

            def lo_hid(m, j, cols, n):
                pool.wait_ge(hid_hi, m + 1)
                pool.tensor_tensor(E_HID[:, j, 1, cols:cols + n], E_H[:, 0:n], E_HID[:, j, 0, cols:cols + n],
                                   ALU.subtract).then_inc(hid_lo, 1)

            def rstd_e(n, s=0):
                pool.wait_ge(e_aggr, n + 1)
                rstd(E_STAT[s]).then_inc(e_rstd, 1)

            with pool.Fori(0, NF) as j:
                for blk in range(2):
                    lo_hid(2 * j + blk, j, BLK * blk, BLK)
            with pool.Fori(0, 8) as j:
                own.enter(j, 0, 1)
                for blk in range(3):
                    lo_hid(2 * NF + 3 * j + blk, j, BLK * blk, BLK if blk < 2 else TS)
                rstd_e(j)
            own.leave(8)
            with pool.Fori(8, NF) as j:
                for blk in range(3):
                    lo_hid(2 * NF + 3 * j + blk, j, BLK * blk, BLK if blk < 2 else TS)
            for n in range(8, NT + 1):
                rstd_e(n, n % 2)

        @block.scalar
        def _(act):
            act.wait_ge(ct_mm, 1)
            act.activation(A_CSIG, ps[:, 6, 0:16], ACT.Sigmoid).then_inc(csig_set, 1)

            def modulate(src_bank, full, t, s, vec, group, done, rows=P):
                for k in range(KD):
                    ins = act.activation(full[:, k * P:k * P + rows],
                                         ps[:, src_bank + k // 4, (k % 4) * P:(k % 4) * P + rows], ACT.Identity,
                                         scale=mod_t[:, vec + 1, k, group:group + 1],
                                         bias=mod_t[:, vec, k, group:group + 1])
                ins.then_inc(done, 1)

            def hi_part(t, full, full_done, hi_done, rows=P):
                act.wait_ge(full_done, t + 1)
                act.activation(hidden_t[:, t, :, 0, 0:rows], full.rearrange("p (k t) -> p k t", k=KD)[:, :, 0:rows],
                               ACT.Identity).then_inc(hi_done, 1)

            def tile_a(t, s, first=False, rows=P, group=0):
                act.wait_ge(a_tr, t + 1)
                if not first:
                    act.wait_ge(a_lo, t - 1)
                modulate(2 * s, A_HF[s], t, s, 0, group, a_full, rows)
                hi_part(t, A_HF[s], a_full, a_hi, rows)

            act.wait_ge(mod_set, 1)
            tile_a(0, 0, True)
            tile_a(1, 1, True)
            with act.Fori(1, 8) as i:
                for s in range(2):
                    tile_a(2 * i + s, s)

            def w_split(c, s):
                act.wait_ge(w_s, c + 1)
                act.activation(B_HL[s][:, 0:KD * P], B_RAW[s], ACT.Identity,
                               scale=c1(C_W + 2 * s)).then_inc(w_hi, 1)

            def evac(c, s, dst, prompt_at=0, sample_at=SEQ):
                for blk in range(5):
                    act.wait_ge(proj_mm, 5 * c + blk + 1)
                    n = BLK if blk < 4 else TS
                    at = prompt_at + BLK * blk if blk < 4 else sample_at
                    act.activation(dst[:, at:at + n], ps[:, blk, 0:n], ACT.Identity,
                                   scale=c1(C_W + 2 * s + 1)).then_inc(proj_out, 1)

            def wpool_evac(g):
                for blk in range(5):
                    m = 5 * g + blk
                    act.wait_ge(wpool_mm, m + 1)
                    n = BLK if blk < 4 else TS
                    act.activation(B_S[g % 2][:, BLK * blk:BLK * blk + n], ps[:, 5 + m % 2, 0:n], ACT.Identity,
                                   scale=c1(C_PSCALE + g)).then_inc(wpool_out, 1)

            w_split(0, 0)
            tile_a(16, 0, False, TS, 1)
            act.wait_ge(misc_in, 64)
            for g in range(4):
                w_split(g + 1, (g + 1) % 2)
                if g:
                    act.wait_ge(pooled_set, g)
                    act.wait_ge(npool_mm, g)
                evac(g, g % 2, B_U, 16, 2080)
                if g:
                    wpool_evac(g - 1)
            def high_part(c, src):
                act.wait_ge(proj_out, 5 * c + 4)
                act.activation(B_THL[c % 2][:, 0, :], src[:, 0:SEQ], ACT.Identity,
                               scale=c1(C_TS + c - 4)).then_inc(t_hi, 1)

            for c in range(4, 8):
                u = c % 2
                w_split(c + 1, 1 - u)
                if c >= 6:
                    act.wait_ge(q_stored[u], 32)
                evac(c, u, B_QT[u])
                high_part(c, B_QT[u])
            wpool_evac(3)
            for s in range(2):
                w_split(9 + s, 1 - s)
                if s == 0:
                    act.wait_ge(rmax_set, 4)
                    act.wait_ge(pool_stored, 64)
                evac(8 + s, s, B_VT[s])
                act.wait_ge(q_stored[s], 64)
                high_part(8 + s, B_VT[s])
            for c in range(10, 16):
                s = c % 2
                if c < 15:
                    w_split(c + 1, 1 - s)
                act.wait_ge(kvt_mm, 5 * (c - 9))
                if c < 12:
                    act.wait_ge(k_stored[s], 32)
                elif c < 14:
                    act.wait_ge(k_stored[s], 64)
                else:
                    act.wait_ge(vmax_set, c - 13)
                evac(c, s, B_VT[s])
                if c < 12:
                    high_part(c, B_VT[s])

            def before(hp, u):
                return (hp, u - 1) if u else (hp - 1, 2 * NU - 1)

            def sigmoids(hp, u, j, first):
                b, kc = UNITS[u % NU]
                par = u % 2
                z = 8 * NU * hp + 4 * u + j
                w = (j + 1) * P if kc == b else BLK
                act.wait_ge(z_mm, z + 1)
                if j == 0 and 1 <= u <= NPIECE and PIECES[u - 1] == "m":
                    act.activation(MOD_ROW[0:2, :], ps[0:2, 0, 256:512], ACT.Identity).then_inc(mod_new, 1)
                if not first or u >= 1:
                    act.wait_ge(scan_set, z - 3)
                if not first or u >= 2:
                    act.wait_ge(prod_set, z - 7)
                act.activation(PRW[:, j, par, 0:w], ps[:, j % 2, 0:w], ACT.Sigmoid,
                               scale=c1(C_ZNOW)).then_inc(sg_set, 1)
                if j == 0 and (not first or u >= 2):
                    act.wait_ge(at_mm, 8 * NU * hp + 4 * u - 4)
                act.activation(C_A[:, par, j, 0:w], ps[:, j % 2, 0:w], ACT.Sigmoid,
                               scale=c1(C_ZNOW + 1)).then_inc(be_set, 1)

            def evac_at(hp, u, kt, first=False):
                b, kc = UNITS[u % NU]
                j0 = kt * P if kc == b else 0
                m = 8 * NU * hp + 4 * u + kt
                act.wait_ge(at_mm, m + 1)
                if not first:
                    act.wait_ge(av_mm, m - 3)
                act.activation(C_AT[kt][:, 0, j0:BLK], ps[:, 2 + kt, j0:BLK], ACT.Identity,
                               scale=2.0 ** TOP).then_inc(at_act, 1)

            def v_split(hp, e, first=False):
                act.wait_ge(v_in[e], 16 * hp + 16)
                if not first:
                    act.wait_ge(av_mm, 8 * NU * (hp - 1) + 4 * NU * (e + 1))
                act.activation(C_VHL[:, e, :, 0:HD], C_VRAW[e], ACT.Identity, scale=c1(C_SMIX)).then_inc(v_hi, 1)

            def head_low(hp, u):
                b, kc = UNITS[u % NU]
                if kc:
                    return
                ob = 8 * hp + 4 * (u // NU) + b
                act.wait_ge(av_mm, 8 * NU * hp + 4 * u + 4)
                if not isinstance(ob, int) or ob:
                    act.wait_ge(o_scaled, ob)
                act.activation(C_OLOW[0:HD, :], ps[HD:P, 6 + b % 2, :], ACT.Identity,
                               scale=2.0 ** -TOP).then_inc(o_low, 1)

            def pair(hp, first=False, last=False):
                if not first:
                    act.wait_ge(be_set, 8 * NU * hp)
                    act.activation(c1(C_SPARE), c1(C_NEGHALF), ACT.Identity)
                act.activation(c1(C_ZNOW, 2), col[:, bass.ds(2 * hp + C_Z, 2)], ACT.Identity).then_inc(z_now, 1)
                act.wait_ge(z_now, hp + 1)
                for u in range(2 * NU):
                    for j in range(4):
                        sigmoids(hp, u, j, first)
                        if not (first and u == 0):
                            evac_at(*before(hp, u), j, first and u == 1)
                        if j == 1 and not (first and u < 2):
                            head_low(*before(*before(hp, u)))
                    if u == 8:
                        v_split(hp, 1, first)
                    if u == 18 and not last:
                        v_split(hp + 1, 0)

            act.wait_ge(mix_set, 1)
            v_split(0, 0, True)
            pair(0, True)
            with act.Fori(1, NPAIR - 1) as hp:
                pair(hp)
            pair(NPAIR - 1, False, True)
            for kt in range(4):
                evac_at(NPAIR - 1, 2 * NU - 1, kt)
            head_low(NPAIR - 1, 2 * NU - 1)
            for g in range(2):
                act.wait_ge(sz_mm, g + 1)
                for dst, sc in ((C_SP[g], -SCALE), (C_SA[g], SCALE)):
                    act.activation(dst[:, 0:PAST], ps[:, 2 * g, 0:PAST], ACT.Sigmoid, scale=sc).then_inc(ssig, 1)
                    act.activation(dst[:, PAST:PAST + TS], ps[:, 2 * g + 1, 0:TS], ACT.Sigmoid, scale=sc).then_inc(ssig, 1)

            act.wait_ge(fin_set, 1)
            for k in range(KD):
                act.wait_ge(wo_raw[k % 4], 16 * (k // 4 + 1))
                act.activation(D_WO[:, 0, k, :], D_RAW[k % 4], ACT.Identity, scale=c1(C_SWO)).then_inc(wo_hi, 1)

            def tile_d(t, s, first=False, rows=P, group=0):
                act.wait_ge(d_tr, t + 1)
                if not first:
                    act.wait_ge(d_lo, t - 1)
                modulate(4 + 2 * s, D_HF[s], t, s, 3, group, d_full, rows)
                hi_part(t, D_HF[s], d_full, d_hi, rows)

            tile_d(0, 0, True)
            tile_d(1, 1, True)
            with act.Fori(1, 7) as i:
                for s in range(2):
                    tile_d(2 * i + s, s)
            tile_d(14, 0)

            def gu_split(n, s, used):
                act.wait_ge(gu_raw, 32 * (n + 1))
                if used is not None:
                    act.wait_ge(gu_mm, used)
                act.activation(E_GHL[s][:, 0, :, :, :], E_GRAW, ACT.Identity, scale=c1(C_SGU)).then_inc(gu_hi, 1)

            def hidden(m, j, blk, cols, n):
                act.wait_ge(gu_mm, m + 1)
                if blk < 2:
                    gate = ps[:, 2 * blk, 0:n]
                else:
                    gate = ps[:, 4, 0:n]
                if not isinstance(m, int) or m:
                    act.wait_ge(hid_set, m)
                act.activation(E_SIG[:, 0:n], gate, ACT.Sigmoid, scale=c1(C_F1)).then_inc(sig_set, 1)
                act.wait_ge(hid_set, m + 1)
                act.activation(E_HID[:, j, 0, cols:cols + n], E_H[:, 0:n], ACT.Identity).then_inc(hid_hi, 1)

            def dn_split(n, h, s, used):
                act.wait_ge(wd_raw, 16 * (n + 1))
                if used is not None:
                    act.wait_ge(dn_mm, used)
                act.activation(E_DHL[s][:, 0, 11 * h:11 * h + 11, :], E_DRAW, ACT.Identity,
                               scale=c1(C_SWD)).then_inc(wd_hi, 1)

            def dn_evac(m, c, grp, blk, src):
                act.wait_ge(dn_mm, m + 1)
                if blk < 2:
                    dst = hidden_t[:, 8 * grp + 4 * blk:8 * grp + 4 * blk + 4, :, :, :].bitcast(f32).rearrange(
                        "p i k a t -> p i (k a t)")
                    act.activation(dst[:, :, bass.ds(c * P, P)], bank(src, BLK, 0), ACT.Identity,
                                   scale=mod_t[:, 5, bass.ds(c, 1), 0:1].rearrange("p a b -> p (a b)")).then_inc(dn_out, 1)
                else:
                    dst = hidden_t[:, NT, :, :, :].bitcast(f32).rearrange("p k a t -> p (k a t)")
                    act.activation(dst[:, bass.ds(c * P, TS)], ps[:, src, 0:TS], ACT.Identity,
                                   scale=mod_t[:, 5, bass.ds(c, 1), 1:2].rearrange("p a b -> p (a b)")).then_inc(dn_out, 1)

            gu_split(0, 0, None)
            tile_d(15, 1)
            tile_d(16, 0, False, TS, 1)
            act.wait_ge(x1_stored[0], 144)
            act.wait_ge(x1_stored[1], 128)

            def chunk(grp, j, s, last=False):
                nb, m0, n0 = 2 + grp, 2 * NF * grp, NF * grp
                if not last:
                    gu_split(n0 + j + 1, 1 - s, m0 + nb * j if not isinstance(j, int) or j else None)
                for blk in range(nb):
                    hidden(m0 + nb * j + blk, j, blk, BLK * blk, BLK if blk < 2 else TS)

            def down(p, c, s, last=False):
                grp, blks, banks, m0 = PASSES[p]
                nb = len(blks)
                if not last:
                    first = isinstance(c, int) and c == 0
                    for h in range(2):
                        dn_split(16 * p + 2 * (c + 1) + h, h, 1 - s,
                                 (m0 if p else None) if first else m0 + nb * c)
                for i, blk in enumerate(blks):
                    dn_evac(m0 + nb * c + i, c, grp, blk, banks[i] if nb > 1 else banks[s])

            for grp in range(2):
                nb = 2 + grp
                if grp:
                    act.wait_ge(dn_mm, 16)
                chunk(grp, 0, 0)
                chunk(grp, 1, 1)
                with act.Fori(1, NF // 2 - 1) as i:
                    for s in range(2):
                        chunk(grp, 2 * i + s, s)
                chunk(grp, NF - 2, 0)
                act.wait_ge(gu_mm, 2 * NF * grp + nb * (NF - 1))
                for h in range(2):
                    dn_split(16 * grp + h, h, 0, None)
                chunk(grp, NF - 1, 1, True)
                act.wait_ge(gu_mm, 2 * NF + 3 * NF * grp)
                passes = (0,) if grp == 0 else (1, 2)
                for p in passes:
                    down(p, 0, 0)
                    down(p, 1, 1)
                    with act.Fori(1, 3) as i:
                        for s in range(2):
                            down(p, 2 * i + s, s)
                    down(p, 6, 0)
                    if p == 0:
                        gu_split(NF, 0, None)
                    if p == 1:
                        for h in range(2):
                            dn_split(32 + h, h, 0, 16 + 14)
                    down(p, 7, 1, True)

        @block.vector
        def _(v):
            own = Steps(v, dve)

            def step(ins):
                own.done(ins)
                own.wait()

            def pow2(src, s, f, n=1):
                t, e2, inv = small[:, 48:48 + n], small[:, 52:52 + n], small[:, 56:56 + n]
                step(v.tensor_scalar(t, src, 1e-30, 1e36, ALU.max, ALU.min))
                step(v.tensor_scalar(e2.bitcast(i32), t.bitcast(i32), 0x7F800000, None, ALU.bitwise_and))
                step(v.tensor_scalar(inv.bitcast(i32), e2.bitcast(i32), -1.0, float(0x7F000000), ALU.mult, ALU.add))
                own.done(v.tensor_scalar(s, inv, 2.0 ** TOP, None, ALU.mult))
                step(v.tensor_scalar(f, e2, 2.0 ** -TOP, None, ALU.mult))

            def abs_max(dst, src):
                return v.tensor_reduce(dst, src, AX.X, ALU.max, apply_absolute_value=True)

            def stats(x, stat, rows, aggr):
                own.done(v.bn_stats(stat[0:rows, 0:6], x[0:rows, 0:512]))
                step(v.bn_stats(stat[0:rows, 6:12], x[0:rows, 512:1024]))
                v.memset(small[:, 64:65], 0.0)
                v.bn_aggr(stat[0:rows, 12:14], stat[0:rows, 0:12]).then_inc(aggr, 1)

            def ln_a(t, s, first=False, rows=P):
                v.wait_ge(x_in[s], t * 8 + 16 - 8 * s)
                stats(A_X[s], A_STAT[s], rows, a_aggr)
                v.wait_ge(a_rstd, t + 1)
                if not first:
                    v.wait_ge(a_tr, t - 1)
                v.tensor_scalar(A_XH[s][0:rows, :], A_X[s][0:rows, :], A_STAT[s][0:rows, 12:13],
                                A_STAT[s][0:rows, 15:16], ALU.subtract, ALU.mult).then_inc(a_xhat, 1)

            for s in range(2):
                own.done(v.memset(A_STAT[s], 1.0))
            own.wait()
            v.wait_ge(csig_set, 1)
            v.tensor_tensor(CT.rearrange("p b k -> p (b k)"), ps[:, 6, 0:16], A_CSIG, ALU.mult).then_inc(ct_set, 1)
            v.wait_ge(ct_mm, 2)
            for b in range(2):
                own.done(v.tensor_copy(mod_t.rearrange("p v k b -> p (v k) b")[:, :, b], ps[:, 7, 64:112]))
            own.wait()

            def mod_scale(vec, top, s_col, f_col, bound):
                flat = [mod_t[:, vec + i, :, :].rearrange("p k b -> p (k b)") for i in range(2)]
                step(v.tensor_tensor(small[:, 4:5], top[:, 0:1], top[:, 1:2], ALU.add))
                step(v.tensor_scalar(c1(bound), small[:, 4:5], LN_ROOT, None, ALU.mult))
                pow2(c1(bound), c1(s_col), c1(f_col))
                own.done(v.tensor_scalar(flat[0], flat[0], c1(s_col), None, ALU.mult))
                return v.tensor_scalar(flat[1], flat[1], c1(s_col), None, ALU.mult)

            def mod_maxima(vec, dst):
                flat = [mod_t[:, vec + i, :, :].rearrange("p k b -> p (k b)") for i in range(2)]
                step(v.tensor_scalar(flat[1], flat[1], 1.0, None, ALU.add))
                own.done(abs_max(dst[:, 0:1], flat[0]))
                return abs_max(dst[:, 1:2], flat[1])

            def ada_rows(s):
                v.wait_ge(ada_mm, s + 1)
                v.tensor_copy(A_MROW[0:2, 512 * s:512 * (s + 1)], ps[0:2, 4 + s % 2, :]).then_inc(ada_row, 1)

            ada_rows(0)
            ada_rows(1)
            ln_a(0, 0, True)
            ada_rows(2)
            ln_a(1, 1, True)
            ada_rows(3)
            v.wait_ge(mod_turned, 1)
            both = mod_t[:, 0:2, :, :].rearrange("p v k b -> p (v k b)")
            step(v.tensor_tensor(both, both, ps[:, 6, 32:64], ALU.add))
            mod_maxima(0, small[:, 0:2]).then_inc(mod_max, 1)
            v.wait_ge(mod_ar, 1)
            mod_scale(0, small[:, 2:4], C_SH, C_FH, C_BOUND).then_inc(mod_set, 1)
            with v.Fori(1, 8) as i:
                own.enter(i, 1, 4)
                for s in range(2):
                    ln_a(2 * i + s, s)
            own.leave(7)

            def prep_max(c):
                s = c % 2
                v.wait_ge(w_in_raw[s], 16 * (c // 2 + 1))
                if c >= 2:
                    v.wait_ge(proj_out, 5 * (c - 1))
                abs_max(small[:, 6 + s:7 + s], B_RAW[s]).then_inc(w_mx, 1)

            def prep_split(c):
                s = c % 2
                v.wait_ge(w_ar, c + 1)
                pow2(small[:, 8 + s:9 + s], c1(C_W + 2 * s), c1(C_W + 2 * s + 1))
                if 4 <= c < 12:
                    step(v.tensor_tensor(small[:, 81:82], small[:, 8 + s:9 + s], c1(C_BOUND), ALU.mult))
                    step(v.tensor_scalar(small[:, 82:83], small[:, 81:82], LN_ROOT, 1e-6, ALU.mult, ALU.max))
                    pow2(small[:, 82:83], c1(C_TS + c - 4), c1(C_TF + c - 4))
                if 8 <= c < 12:
                    pair = c - 8
                    step(v.tensor_tensor(small[:, 83:84], c1(C_TF + pair), c1(C_TF + 4 + pair), ALU.mult))
                    for i, sign in enumerate((-SCALE, SCALE)):
                        own.done(v.tensor_scalar(c1(C_Z + 2 * pair + i), small[:, 83:84], sign, None, ALU.mult))
                v.tensor_tensor(c1(C_W + 2 * s + 1), c1(C_W + 2 * s + 1), c1(C_FH), ALU.mult).then_inc(w_s, 1)
                v.wait_ge(w_hi, c + 1)
                v.scalar_tensor_tensor(B_HL[s][:, KD * P:2 * KD * P], B_RAW[s], c1(C_W + 2 * s),
                                       B_HL[s][:, 0:KD * P], ALU.mult, ALU.subtract).then_inc(w_lo, 1)

            def pool_rows(g):
                win = 2 ** (g + 1)
                v.wait_ge(proj_out, 5 * (g + 1))
                step(v.tensor_copy(B_U[:, 2065:2080], HIST_T[:, HIST * g:HIST * (g + 1)]))
                if g:
                    v.wait_ge(pool_stored, 16 * g)
                src = B_U
                for i in range(g + 1):
                    d, dst = 2 ** i, B_S[i % 2]
                    st = 2 * d - 1
                    step(v.tensor_tensor(dst[:, st:UW], src[:, st:UW], src[:, st - d:UW - d], ALU.add))
                    src = dst
                dst = B_S[(g + 1) % 2]
                first = 16 + win - 1
                own.done(v.scalar_tensor_tensor(dst[:, first:UW], src[:, first:UW], 1.0 / win,
                                                B_U[:, first:UW], ALU.mult, ALU.subtract))
                step(v.tensor_tensor(dst[:, 16:first], src[:, 16:first], c1(C_INV, win - 1), ALU.mult))
                v.tensor_tensor(dst[:, 16:first], dst[:, 16:first], B_U[:, 16:first],
                                ALU.subtract).then_inc(pooled_set, 1)

            def last_rows(g):
                v.wait_ge(npool_mm, g + 1)
                v.tensor_copy(B_NPOOL[0:HIST, :].rearrange("p (b n) -> p b n", b=2)[:, :, g * P:(g + 1) * P],
                              ps[0:HIST, 7, 0:2 * P].rearrange("p (b n) -> p b n", b=2)).then_inc(npool_out, 1)

            def pool_max(g):
                v.wait_ge(wpool_out, 5 * (g + 1))
                abs_max(c1(C_POOLMAX + g), B_S[g % 2][:, 0:TOK]).then_inc(rmax_set, 1)

            def low_part(c, src):
                v.wait_ge(t_hi, c - 3)
                v.scalar_tensor_tensor(B_THL[c % 2][:, 1, :], src[:, 0:SEQ], c1(C_TS + c - 4), B_THL[c % 2][:, 0, :],
                                       ALU.mult, ALU.subtract).then_inc(t_lo, 1)

            def rows_out(c):
                for g in range(5):
                    m = 5 * (c - 8) + g
                    slot = m % 2
                    v.wait_ge(kvt_mm, m + 1)
                    if m >= 2:
                        v.wait_ge(kv_stored[slot], 16 * (m // 2))
                    n, rows = (BLK, P) if g < 4 else (P, TS)
                    v.tensor_copy(B_STG[slot][0:rows, 0:n], ps[0:rows, 5 + slot, 0:n]).then_inc(kvt_out, 1)

            prep_max(0)
            ln_a(16, 0, False, TS)
            v.wait_ge(hist_mm, 1)
            step(v.tensor_copy(HIST_T, ps[:, 7, 0:4 * HIST]))
            own.done(v.memset(B_U[:, 0:16], 0.0))
            step(v.memset(B_U[:, 2064:2065], 0.0))
            prep_split(0)
            for c in range(16):
                if c < 15:
                    prep_max(c + 1)
                    prep_split(c + 1)
                if 1 <= c <= 3:
                    pool_max(c - 1)
                if c < 4:
                    pool_rows(c)
                    last_rows(c)
                if c == 8:
                    pool_max(3)
                if c >= 9:
                    rows_out(c - 1)
                if 4 <= c < 12:
                    low_part(c, B_QT[c % 2] if c < 8 else B_VT[c % 2])
                if c == 11:
                    v.wait_ge(cv_in, 16)
                    step(abs_max(c1(C_VMAX + 4), B_CV))
                if c >= 12:
                    v.wait_ge(proj_out, 5 * (c + 1))
                    abs_max(c1(C_VMAX + c - 12), B_VT[c % 2]).then_inc(vmax_set, 1)
            rows_out(15)
            v.wait_ge(vmax_set, 4)
            v.wait_ge(rmax_set, 4)
            v.tensor_reduce(small[:, 43:44], c1(C_POOLMAX, 9), AX.X, ALU.max).then_inc(mix_max, 1)
            v.wait_ge(mix_ar, 1)
            pow2(small[:, 47:48], c1(C_SMIX), c1(C_FMIX))
            v.memset(small[:, 64:65], 0.0).then_inc(mix_set, 1)
            for s in range(2):
                v.wait_ge(kv_stored[s], 320)
            v.wait_ge(out_small, 32)
            v.wait_ge(wpool_mm, 20)
            for s in range(2):
                v.wait_ge(q_stored[s], 64)
            v.memset(C_PIECE[0][:, 0:1], 0.0).then_inc(piece_free, 1)
            v.memset(C_PIECE[1][:, 0:1], 0.0).then_inc(piece_free, 1)

            def pool_parts(hp):
                parts = [(C_PIECE[0][:, 0:SEQ].rearrange("p (i t) -> p i t", t=P),
                          [hidden_t[:, 0:NT, hp, h, :] for h in range(2)]),
                         (C_PIECE[0][:, SEQ:TOK], [hidden_t[:, NT, hp, h, 0:TS] for h in range(2)])]
                for src, (hi, lo) in parts:
                    own.done(v.tensor_scalar(hi, src, c1(C_SMIX), None, ALU.mult))
                own.wait()
                for n, (src, (hi, lo)) in enumerate(parts):
                    ins = v.scalar_tensor_tensor(lo, src, c1(C_SMIX), hi, ALU.mult, ALU.subtract)
                    if n == 0:
                        own.done(ins)
                return ins

            def piece(hp, i):
                s = i % 2
                kind = PIECES[i]
                if kind == "m":
                    rows = mod_t[:, hp + 2, 2 * place(i):2 * place(i) + 2, :]
                    ins = v.tensor_tensor(rows, rows, ps[:, 3, 0:4].rearrange("p (k b) -> p k b", b=2), ALU.add)
                else:
                    v.wait_ge(piece_in[s], NPIECE // 2 * 16 * hp + 16 * (i // 2 + 1))
                    if kind == "a":
                        ins = pool_parts(hp)
                    else:
                        m = MAX_OF.index(i)
                        ins = abs_max(NEW_MAX[:, m:m + 1], C_PIECE[s][:, 0:PIECE_N[kind]])
                ins.then_inc(piece_free, 1)

            def scan(hp, u, j):
                b, kc = UNITS[u % NU]
                par = u % 2
                if kc == b and j == 0:
                    step(v.memset(C_PR[:, par * PB + P:par * PB + P + 3 * (2 * PB + P) + 1:2 * PB + P], 1.0))
                z = 8 * NU * hp + 4 * u + j
                w = (j + 1) * P if kc == b else BLK
                v.wait_ge(sg_set, z + 1)
                row = PRW[:, j, par, w - 1::-1]
                v.tensor_tensor_scan(row, row, row, PRW[:, j, par, w:w + 1],
                                     ALU.mult, ALU.bypass).then_inc(scan_set, 1)

            def pass_edge(hp, u, first):
                par = u % 2
                v.wait_ge(scan_set, 8 * NU * hp + 4 * u + 4)
                if not first or u:
                    v.wait_ge(prod_set, 8 * NU * hp + 4 * u)
                step(v.tensor_copy(PRW[:, :, 1 - par, BLK:BLK + 1], PRW[:, :, par, 0:1]))

            def evac_at_dve(hp, u, kt, first=False):
                b, kc = UNITS[u % NU]
                j0 = kt * P if kc == b else 0
                m = 8 * NU * hp + 4 * u + kt
                v.wait_ge(at_act, m + 1)
                v.scalar_tensor_tensor(C_AT[kt][:, 1, j0:BLK], ps[:, 2 + kt, j0:BLK], 2.0 ** TOP,
                                       C_AT[kt][:, 0, j0:BLK], ALU.mult, ALU.subtract).then_inc(at_dve, 1)

            def v_low(hp, e):
                v.wait_ge(v_hi, 2 * hp + e + 1)
                v.scalar_tensor_tensor(C_VHL[:, e, :, HD:P], C_VRAW[e], c1(C_SMIX), C_VHL[:, e, :, 0:HD],
                                       ALU.mult, ALU.subtract).then_inc(v_lo, 1)

            def head_out(hp, u):
                b, kc = UNITS[u % NU]
                if kc:
                    return
                e = u // NU
                r = slice(HD * e, HD * e + HD)
                ob = 8 * hp + 4 * e + b
                v.wait_ge(o_low, ob + 1)
                v.scalar_tensor_tensor(C_ST[b % 2][r, :], ps[0:HD, 6 + b % 2, :], 2.0 ** -TOP, C_OLOW[0:HD, :],
                                       ALU.mult, ALU.add).then_inc(o_scaled, 1)
                v.wait_ge(o_scaled, ob + 1)
                st = C_ST[b % 2][r, :].rearrange("p (i t) -> p i t", t=P)
                dst = [hidden_t[r, 4 * b:4 * b + 4, 4 + hp, h, :] for h in range(2)]
                step(v.tensor_copy(dst[0], st))
                v.tensor_tensor(dst[1], st, dst[0], ALU.subtract).then_inc(o_split, 1)

            def pair(hp, first=False, last=False):
                def back(u, n):
                    return (hp, u - n) if u >= n else (hp - 1, 2 * NU + u - n)

                for u in range(2 * NU):
                    i = u - 1
                    for j in range(4):
                        scan(hp, u, j)
                        if not (first and u == 0):
                            if j == 1 and i >= 1 and PIECES[i - 1] == "m":
                                v.wait_ge(at_act, 8 * NU * hp + 4 * i + 2)
                                piece(hp, i - 1)
                            evac_at_dve(*back(u, 1), j, first and u == 1)
                        if j == 1 and not (first and u < 2):
                            head_out(*back(u, 2))
                    pass_edge(hp, u, first)
                    if u == 8:
                        v_low(hp, 1)
                    if u == 18 and not last:
                        v_low(hp + 1, 0)
                    if 0 <= i < NPIECE and PIECES[i] != "m":
                        piece(hp, i)
                v.wait_ge(piece_free, NPIECE * hp + NPIECE + 2)
                step(v.tensor_tensor(ALL_MAX, ALL_MAX, NEW_MAX, ALU.max))

            v_low(0, 0)
            pair(0, True)
            with v.Fori(1, NPAIR - 1) as hp:
                own.enter(hp, 1, 40)
                pair(hp)
            own.leave(NPAIR - 2)
            pair(NPAIR - 1, False, True)
            for kt in range(4):
                evac_at_dve(NPAIR - 1, 2 * NU - 1, kt)
            head_out(NPAIR - 1, 2 * NU - 1)

            for hp in range(NPAIR):
                v.wait_ge(ck_mm, hp + 1)
                v.tensor_copy(C_CKT[:, hp, :], ps[:, 4 + hp % 2, :]).then_inc(ck_set, 1)

            top = small[:, 86:91]
            for m, (kind, n) in enumerate((("g", 8), ("d", 4), ("o", 1))):
                at = [PIECES[i] for i in MAX_OF].index(kind)
                own.done(v.tensor_reduce(top[:, m:m + 1], ALL_MAX[:, at:at + n], AX.X, ALU.max))
            mod_maxima(3, top[:, 3:5]).then_inc(fin_max, 1)
            v.wait_ge(fin_ar, 1)
            top = small[:, 91:96]
            step(mod_scale(3, top[:, 3:5], C_SH2, C_FH2, C_BOUND + 1))
            pow2(top[:, 0:3], c1(C_SGU, 3), c1(C_FGU, 3), 3)
            step(v.tensor_tensor(small[:, 60:61], c1(C_BOUND + 1), top[:, 0:1], ALU.mult))
            step(v.tensor_scalar(small[:, 61:62], small[:, 60:61], LN_ROOT, None, ALU.mult))
            step(v.tensor_tensor(small[:, 62:63], small[:, 61:62], small[:, 61:62], ALU.mult))
            pow2(small[:, 62:63], c1(C_SHID), c1(C_FHID))
            own.done(v.tensor_tensor(c1(C_FWOMIX), c1(C_FWO), c1(C_FMIX), ALU.mult))
            own.done(v.tensor_tensor(c1(C_FDOWN), c1(C_FWD), c1(C_FHID), ALU.mult))
            step(v.tensor_tensor(c1(C_F1), c1(C_FGU), c1(C_FH2), ALU.mult))
            own.done(v.tensor_tensor(c1(C_F2), c1(C_F1), c1(C_SHID), ALU.mult))
            g2 = mod_t[:, 5, :, :].rearrange("p k b -> p (k b)")
            v.tensor_scalar(g2, g2, c1(C_FDOWN), None, ALU.mult).then_inc(fin_set, 1)
            v.wait_ge(fin_set, 1)

            W1 = PAST + TS

            def wo_low(chunks):
                for k in chunks:
                    v.wait_ge(wo_hi, k + 1)
                    v.scalar_tensor_tensor(D_WO[:, 1, k, :], D_RAW[k % 4], c1(C_SWO), D_WO[:, 0, k, :],
                                           ALU.mult, ALU.subtract).then_inc(wo_lo, 1)

            for g in range(2):
                step(v.memset(C_SP[g][:, W1:W1 + 1], 1.0))
                v.wait_ge(ssig, 4 * (g + 1))
                row = C_SP[g][:, W1 - 1::-1]
                step(v.tensor_tensor_scan(row, row, row, 1.0, ALU.mult, ALU.bypass))
                v.tensor_tensor(C_SA[g][:, 0:W1], C_SA[g][:, 0:W1], C_SP[g][:, 1:W1 + 1],
                                ALU.mult).then_inc(sprod, 1)
            wo_low(range(2))
            for g in range(2):
                v.wait_ge(sat_mm, g + 1)
                v.tensor_copy(C_SAT[g][:, 0:512], ps[:, 4 + g, :]).then_inc(sat_set, 1)
                v.tensor_copy(C_SAT[g][0:TS, 512:640], ps[0:TS, 6 + g, 0:P]).then_inc(sat_set, 1)
            wo_low(range(2, 4))
            v.wait_ge(so_mm, 1)
            step(v.tensor_scalar(C_SST, ps[:, 0, 0:P], c1(C_SMIX), None, ALU.mult))
            st = C_SST.rearrange("p (h t) -> p h t", h=4)
            step(v.tensor_copy(hidden_t[:, NT, 4:8, 0, 0:TS], st))
            v.tensor_tensor(hidden_t[:, NT, 4:8, 1, 0:TS], st, hidden_t[:, NT, 4:8, 0, 0:TS],
                            ALU.subtract).then_inc(so_split, 1)

            step(v.memset(D_ONES, 1.0))
            for b in range(2):
                for k in range(KD):
                    v.tensor_scalar(D_REP[:, b, k, :], D_ONES, mod_t[:, 2, k, b:b + 1], None,
                                    ALU.mult).then_inc(g1_rep, 1)
            for b in range(2):
                for n in range(2):
                    v.wait_ge(g1_mm, 2 * b + n + 1)
                    v.tensor_scalar(D_G1[:, b, 512 * n:512 * (n + 1)], ps[:, 4 + 2 * b + n, :], c1(C_FWOMIX), None,
                                    ALU.mult).then_inc(g1_set, 1)
            wo_low(range(4, KD))
            v.wait_ge(ln1_in, 32)
            v.wait_ge(g1_set, 4)
            for s in range(2):
                own.done(v.memset(D_STAT[s], 1.0))
            own.wait()

            def tile_d(t, s, xin, first=False, rows=P, group=0):
                r = slice(0, rows)
                stat = D_STAT[s]
                v.wait_ge(d_mm, t + 1)
                v.tensor_tensor(D_R[s][r, :], ps[r, 2 * s:2 * s + 2, :].rearrange("p a n -> p (a n)"),
                                D_G1[r, group, :], ALU.mult).then_inc(d_mo, 1)
                v.wait_ge(d_mo, t + 1)
                v.wait_ge(dx_in[s], xin)
                v.scalar_tensor_tensor(D_R[s][r, :], D_X[s][r, :], ALPHA, D_R[s][r, :],
                                       ALU.mult, ALU.add).then_inc(d_res, 1)
                v.wait_ge(d_res, t + 1)
                stats(D_R[s], stat, rows, d_aggr1)
                v.wait_ge(d_rstd1, t + 1)
                step(v.scalar_tensor_tensor(D_R[s][r, :], D_R[s][r, :], stat[r, 12:13], D_LN1[r, 0, :],
                                            ALU.subtract, ALU.mult))
                if not first:
                    v.wait_ge(x1_stored[s], xin - 16)
                    v.wait_ge(d_tr, t - 1)
                v.scalar_tensor_tensor(D_X1[s][r, :], D_R[s][r, :], stat[r, 15:16], D_LN1[r, 1, :],
                                       ALU.mult, ALU.add).then_inc(d_x1, 1)
                v.wait_ge(d_x1, t + 1)
                stats(D_X1[s], stat, rows, d_aggr2)
                v.wait_ge(d_rstd2, t + 1)
                v.tensor_scalar(D_XH[s][r, :], D_X1[s][r, :], stat[r, 12:13], stat[r, 15:16],
                                ALU.subtract, ALU.mult).then_inc(d_xhat, 1)

            tile_d(0, 0, 16, True)
            tile_d(1, 1, 16, True)
            with v.Fori(1, 8) as i:
                own.enter(i, 1, 10)
                for s in range(2):
                    tile_d(2 * i + s, s, 16 * i + 16)
            own.leave(7)


            def gu_low(n, s):
                v.wait_ge(gu_hi, n + 1)
                v.scalar_tensor_tensor(E_GHL[s][:, 1, :, :, :].rearrange("p k w n -> p (k w n)"),
                                       E_GRAW.rearrange("p k w n -> p (k w n)"), c1(C_SGU),
                                       E_GHL[s][:, 0, :, :, :].rearrange("p k w n -> p (k w n)"),
                                       ALU.mult, ALU.subtract).then_inc(gu_lo, 1)

            def hidden(m, blk, n):
                gate = ps[:, 2 * blk, 0:n] if blk < 2 else ps[:, 4, 0:n]
                up = ps[:, 2 * blk + 1, 0:n] if blk < 2 else ps[:, 4, TS:2 * TS]
                v.wait_ge(sig_set, m + 1)
                step(v.scalar_tensor_tensor(E_T[:, 0:n], gate, c1(C_F1), E_SIG[:, 0:n], ALU.mult, ALU.mult))
                if not isinstance(m, int) or m:
                    v.wait_ge(hid_lo, m)
                v.scalar_tensor_tensor(E_H[:, 0:n], up, c1(C_F2), E_T[:, 0:n],
                                       ALU.mult, ALU.mult).then_inc(hid_set, 1)

            def ln2(n, s=0, rows=P):
                r = slice(0, rows)
                x, stat, at = E_X1[s], E_STAT[s], 5 - 2 * s
                v.wait_ge(e_x1[s], 16 * (ln2_uses(n) if isinstance(n, int) else n + 1))
                v.wait_ge(e_tr, n + 1)
                v.scalar_tensor_tensor(x[r, :], x[r, :], ALPHA, ps[r, at:at + 2, :].rearrange("p a n -> p (a n)"),
                                       ALU.mult, ALU.add).then_inc(e_res, 1)
                v.wait_ge(e_res, n + 1)
                stats(x, stat, rows, e_aggr)
                v.wait_ge(e_rstd, n + 1)
                step(v.scalar_tensor_tensor(x[r, :], x[r, :], stat[r, 12:13], ln2_rows[r, 0, :],
                                            ALU.subtract, ALU.mult))
                v.scalar_tensor_tensor(x[r, :], x[r, :], stat[r, 15:16], ln2_rows[r, 1, :],
                                       ALU.mult, ALU.add).then_inc(e_y, 1)

            def dn_low(n, h, s):
                v.wait_ge(wd_hi, n + 1)
                parts = [E_DHL[s][:, i, 11 * h:11 * h + 11, :].rearrange("p j n -> p (j n)") for i in range(2)]
                v.scalar_tensor_tensor(parts[1], E_DRAW.rearrange("p j n -> p (j n)"), c1(C_SWD), parts[0],
                                       ALU.mult, ALU.subtract).then_inc(wd_lo, 1)

            def chunk(grp, j, s, last=False, with_ln=False):
                nb, m0, n0 = 2 + grp, 2 * NF * grp, NF * grp
                if not last:
                    gu_low(n0 + j + 1, 1 - s)
                for blk in range(nb):
                    hidden(m0 + nb * j + blk, blk, BLK if blk < 2 else TS)
                if with_ln:
                    ln2(j)

            gu_low(0, 0)
            tile_d(16, 0, 144, False, TS, 1)
            v.wait_ge(misc_in, 64)
            step(v.memset(E_STAT[0], 1.0))
            for grp in range(2):
                chunk(grp, 0, 0, False, grp == 1)
                chunk(grp, 1, 1, False, grp == 1)
                if grp == 0:
                    with v.Fori(1, NF // 2 - 1) as i:
                        own.enter(i, 1, 4)
                        for s in range(2):
                            chunk(grp, 2 * i + s, s)
                    own.leave(NF // 2 - 2)
                else:
                    with v.Fori(1, 4) as i:
                        own.enter(i, 1, 12)
                        for s in range(2):
                            chunk(grp, 2 * i + s, s, False, True)
                    own.leave(3)
                    with v.Fori(4, NF // 2 - 1) as i:
                        own.enter(i, 4, 6)
                        for s in range(2):
                            chunk(grp, 2 * i + s, s)
                    own.leave(NF // 2 - 5)
                chunk(grp, NF - 2, 0)
                for h in range(2):
                    dn_low(16 * grp + h, h, 0)
                chunk(grp, NF - 1, 1, True)
                dn_low(16 * grp + 2, 0, 1)
                dn_low(16 * grp + 3, 1, 1)
                with v.Fori(1, KD // 2) as i:
                    for s in range(2):
                        for h in range(2):
                            dn_low(16 * grp + 4 * i + 2 * s + h, h, s)
                if grp == 0:
                    gu_low(NF, 0)
            for h in range(2):
                dn_low(32 + h, h, 0)
            v.wait_ge(hid_lo, 5 * NF)
            step(v.memset(E_STAT[1], 1.0))
            for c in range(KD):
                if c < KD - 1:
                    for h in range(2):
                        dn_low(32 + 2 * (c + 1) + h, h, (c + 1) % 2)
                if c < 5:
                    ln2(8 + c, c % 2, TS if LN2_TILES[8 + c] == NT else P)
            for n in range(13, NT + 1):
                ln2(n, n % 2)

        @block.tensor
        def _(pe):
            pe.wait_ge(consts_set, 1)
            pe.wait_ge(crow_in, 32)
            pe.transpose(ps[:, 6, 0:16], A_CROW[0:16, :], ident[0:16, 0:16]).then_inc(ct_mm, 1)
            pe.wait_ge(brow_in, 16)
            pe.transpose(ps[:, 7, 64:112], A_BROW[0:48, :], ident[0:48, 0:48]).then_inc(ct_mm, 1)

            def turn(t, s, src, ready, done, bank0, free, first=False, rows=P):
                pe.wait_ge(ready, t + 1)
                if not first:
                    pe.wait_ge(free, t - 1)
                for k in range(KD):
                    mm = pe.transpose(ps[:, bank0 + 2 * s + k // 4, (k % 4) * P:(k % 4) * P + rows],
                                      src[s][0:rows, k * P:(k + 1) * P], ident[0:rows, 0:rows])
                mm.then_inc(done, 1)

            pe.wait_ge(ct_set, 1)
            for s in range(4):
                pe.wait_ge(wada_in[s], 16)
                if s >= 2:
                    pe.wait_ge(ada_row, s - 1)
                for k in range(KD):
                    mm = pe.matmul(ps[0:2, 4 + s % 2, :], CT[:, :, k], A_WADA[:, s, k, :],
                                   start=(k == 0), stop=(k == KD - 1))
                mm.then_inc(ada_mm, 1)
            pe.wait_ge(ada_row, 4)
            for q in range(16):
                mm = pe.transpose(ps[:, 6, 32 + 2 * q:34 + 2 * q], A_MROW[0:2, q * P:(q + 1) * P], ident[0:2, 0:2])
            mm.then_inc(mod_turned, 1)
            turn(0, 0, A_XH, a_xhat, a_tr, 0, a_full, True)
            turn(1, 1, A_XH, a_xhat, a_tr, 0, a_full, True)
            with pe.Fori(1, 8) as i:
                for s in range(2):
                    turn(2 * i + s, s, A_XH, a_xhat, a_tr, 0, a_full)
            pe.wait_ge(hist_in, 16)
            for g in range(4):
                mm = pe.transpose(ps[:, 7, HIST * g:HIST * (g + 1)], A_HISTROW[0:HIST, P * g:P * (g + 1)],
                                  ident[0:HIST, 0:HIST])
            mm.then_inc(hist_mm, 1)
            turn(16, 0, A_XH, a_xhat, a_tr, 0, a_full, False, TS)

            pe.wait_ge(a_hi, NT + 1)
            pe.wait_ge(a_lo, NT + 1)
            pe.wait_ge(a_full, NT + 1)

            def project(c, s, first=False, beside=None):
                pe.wait_ge(w_hi, c + 1)
                pe.wait_ge(w_lo, c + 1)
                for blk in range(5):
                    if not first:
                        pe.wait_ge(proj_out, 5 * c + blk - 4)
                    n = BLK if blk < 4 else TS
                    for k in range(KD):
                        for wh, xh in TERMS:
                            mm = pe.matmul(bank(blk, n, blk), B_HL[s][:, wh * KD * P + k * P:wh * KD * P + (k + 1) * P],
                                           moving(k, xh, blk), start=(k == 0 and (wh, xh) == (0, 0)),
                                           stop=(k == KD - 1 and (wh, xh) == TERMS[-1]))
                    mm.then_inc(proj_mm, 1)
                    if beside is not None:
                        token_rows(*beside, blk)

            def mix_pool(g):
                pe.wait_ge(pooled_set, g + 1)
                for blk in range(5):
                    m = 5 * g + blk
                    if m >= 2:
                        pe.wait_ge(wpool_out, m - 1)
                    at, n = (16 + BLK * blk, BLK) if blk < 4 else (2080, TS)
                    pe.matmul(ps[:, 5 + m % 2, 0:n], B_WPOOL[:, g * P:(g + 1) * P],
                              B_S[(g + 1) % 2][:, at:at + n], start=True, stop=True).then_inc(wpool_mm, 1)

            def last_rows(g):
                pe.wait_ge(proj_out, 5 * (g + 1))
                if g:
                    pe.wait_ge(npool_out, g)
                for b, at in enumerate((16 + SEQ - HIST, 2080 + TS - HIST)):
                    mm = pe.transpose(ps[0:HIST, 7, b * P:(b + 1) * P], B_U[:, at:at + HIST], ident[:, :])
                mm.then_inc(npool_mm, 1)

            def token_rows(c, s, g):
                m = 5 * c + g
                par = (s + g) % 2
                pe.wait_ge(proj_out, 5 * c + g + 41)
                if not isinstance(m, int) or m >= 2:
                    pe.wait_ge(kvt_out, m - 1)
                if g < 4:
                    for i in range(4):
                        at = (4 * g + i) * P
                        mm = pe.transpose(ps[:, 5 + par, i * P:(i + 1) * P], B_VT[s][:, at:at + P], ident[:, :])
                else:
                    mm = pe.transpose(ps[0:TS, 5 + par, 0:P], B_VT[s][:, SEQ:TOK], ident[:, :])
                mm.then_inc(kvt_mm, 1)

            pe.wait_ge(misc_in, 64)
            for g in range(4):
                project(g, g % 2, g == 0)
                last_rows(g)
                if g:
                    mix_pool(g - 1)
            with pe.Fori(0, 2) as i:
                for s in range(2):
                    project(2 * i + s + 4, s)
            mix_pool(3)
            pe.wait_ge(wpool_out, 20)
            project(8, 0)
            project(9, 1, False, (0, 0))
            with pe.Fori(1, 4) as i:
                for s in range(2):
                    project(2 * i + s + 8, s, False, (2 * i + s - 1, 1 - s))
            for g in range(5):
                token_rows(7, 1, g)

            def scores(hp, u, j, first=False):
                b, kc = UNITS[u % NU]
                e = u // NU
                z = 8 * NU * hp + 4 * u + j
                w = (j + 1) * P if kc == b else BLK
                qt = (4 * b + j) * P
                if not first or j >= 2:
                    pe.wait_ge(be_set, z - 1)
                if j == 0 and 1 <= u <= NPIECE and PIECES[u - 1] == "m":
                    i = u - 1
                    pe.wait_ge(piece_in[i % 2], NPIECE // 2 * 16 * hp + 16 * (i // 2 + 1))
                    w = C_PIECE[i % 2][:, 0:2048].rearrange("p (k n) -> p k n", k=KD)
                    for k in range(KD):
                        pe.matmul(ps[0:2, 0, 256:512], CT[:, :, k], w[:, k, :], start=(k == 0), stop=(k == KD - 1))
                    w = P
                for h in range(2):
                    mm = pe.matmul(ps[:, j % 2, 0:w], C_Q[e][:, qt:qt + P], C_K[e][:, h, BLK * kc:BLK * kc + w],
                                   start=(h == 0), stop=(h == 1))
                if kc == b:
                    mm = pe.matmul(ps[:, j % 2, w - P:w], ident_b[:, :], mask_b[:, :], start=False, stop=True,
                                   skip_group_check=True)
                mm.then_inc(z_mm, 1)

            def turn_weights(hp, u, kt, first=False):
                b, kc = UNITS[u % NU]
                par = u % 2
                j0 = kt if kc == b else 0
                m = 8 * NU * hp + 4 * u + kt
                if kt == 0:
                    pe.wait_ge(prod_set, 8 * NU * hp + 4 * u + 4)
                if not first:
                    pe.wait_ge(at_dve, m - 3)
                modulated = kt == 1 and 1 <= u <= NPIECE and PIECES[u - 1] == "m"
                if modulated:
                    pe.wait_ge(mod_new, 4 * hp + place(u - 1) + 1)
                for j in range(j0, 4):
                    mm = pe.transpose(ps[:, 2 + kt, j * P:(j + 1) * P], C_A[:, par, j, kt * P:(kt + 1) * P], ident[:, :])
                if modulated:
                    for q in range(2):
                        mm = pe.transpose(ps[:, 3, 2 * q:2 * q + 2], MOD_ROW[0:2, q * P:(q + 1) * P], ident[0:2, 0:2])
                mm.then_inc(at_mm, 1)

            def weigh(hp, u, kt, first=False):
                b, kc = UNITS[u % NU]
                e = u // NU
                j0 = kt * P if kc == b else 0
                pe.wait_ge(at_dve, 8 * NU * hp + 4 * u + kt + 1)
                if u % NU == 0 and kt == 0:
                    pe.wait_ge(v_lo, 2 * hp + e + 1)
                if kc == b and kt == 0 and not first:
                    pe.wait_ge(o_scaled, 8 * hp + 4 * e + b - 1)
                pe.matmul(ps[:, 6 + b % 2, j0:BLK], C_VHL[:, e, 4 * kc + kt, :], C_AT[kt][:, 0, j0:BLK],
                          start=(kc == b and kt == 0), stop=(kc == 0 and kt == 3), skip_group_check=True)
                pe.matmul(ps[0:HD, 6 + b % 2, j0:BLK], C_VHL[:, e, 4 * kc + kt, 0:HD], C_AT[kt][:, 1, j0:BLK],
                          start=False, stop=(kc == 0 and kt == 3), skip_group_check=True).then_inc(av_mm, 1)

            def pair(hp, first=False, last=False):
                for u in range(2 * NU):
                    if u == NU - 1:
                        pe.wait_ge(head_in[1], 64 * hp + 64)
                    if u == 2 * NU - 1 and not last:
                        pe.wait_ge(head_in[0], 64 * hp + 128)

                    def next_scores(j):
                        if u < 2 * NU - 1:
                            scores(hp, u + 1, j)
                        elif not last:
                            scores(hp + 1, 0, j)

                    new = first and u == 0
                    next_scores(0)
                    turn_weights(hp, u, 0, new)
                    next_scores(1)
                    turn_weights(hp, u, 1, new)
                    next_scores(2)
                    weigh(hp, u, 0, first and u < 3)
                    turn_weights(hp, u, 2, new)
                    next_scores(3)
                    weigh(hp, u, 1)
                    turn_weights(hp, u, 3, new)
                    weigh(hp, u, 2)
                    weigh(hp, u, 3)

            pe.wait_ge(head_in[0], 64)
            for j in range(4):
                scores(0, 0, j, True)
            pe.wait_ge(kvt_out, 40)
            pe.wait_ge(npool_out, 4)
            pair(0, True)
            with pe.Fori(1, NPAIR - 1) as hp:
                pair(hp)
            pair(NPAIR - 1, False, True)
            pe.wait_ge(smp_in, 64)
            pe.wait_ge(at_dve, 8 * NU * NPAIR)
            for hp in range(NPAIR):
                if hp >= 2:
                    pe.wait_ge(ck_set, hp - 1)
                for i in range(4):
                    mm = pe.transpose(ps[:, 4 + hp % 2, i * P:(i + 1) * P], C_CK[:, i, hp * P:(hp + 1) * P], ident[:, :])
                mm.then_inc(ck_mm, 1)
            pe.wait_ge(ck_set, 4)
            pe.wait_ge(be_set, 8 * NU * NPAIR)
            for g in range(2):
                for i in range(4):
                    h = 4 * g + i
                    r = slice(HD * (h % 2), HD * (h % 2) + HD)
                    o = slice(TS * i, TS * i + TS)
                    pe.matmul(ps[o, 2 * g, 0:PAST], C_QS[r, h // 2, :], C_CKT[r, h // 2, :], start=True, stop=True)
                    pe.matmul(ps[o, 2 * g + 1, 0:TS], C_QS[r, h // 2, :], C_KS[r, h // 2, :], start=True, stop=False)
                    mm = pe.matmul(ps[o, 2 * g + 1, 0:TS], ident_b[0:TS, 0:TS], mask_b[0:TS, 0:TS],
                                   start=False, stop=True)
                mm.then_inc(sz_mm, 1)
            pe.wait_ge(o_scaled, 8 * NPAIR)
            for g in range(2):
                pe.wait_ge(sprod, g + 1)
                for i in range(4):
                    pe.transpose(ps[:, 4 + g, i * P:(i + 1) * P], C_SA[g][:, i * P:(i + 1) * P], ident[:, :])
                pe.transpose(ps[0:TS, 6 + g, 0:P], C_SA[g][:, PAST:PAST + TS], ident[:, :]).then_inc(sat_mm, 1)
            pe.wait_ge(sat_set, 4)
            pe.wait_ge(ssig, 8)
            cv = B_CV.rearrange("p (i c) -> p i c", c=512)
            for h in range(NH):
                g, i, hp = h // 4, h % 4, h // 2
                r = slice(HD * (h % 2), HD * (h % 2) + HD)
                for kt in range(5):
                    if kt < 4:
                        lhs, rhs = cv[:, kt, h * HD:(h + 1) * HD], C_SAT[g][:, kt * P + TS * i:kt * P + TS * (i + 1)]
                    else:
                        lhs, rhs = C_VN[0:TS, h * HD:(h + 1) * HD], C_SAT[g][0:TS, 512 + TS * i:512 + TS * (i + 1)]
                    mm = pe.matmul(ps[r, 0, hp * TS:(hp + 1) * TS], lhs, rhs, start=(kt == 0), stop=(kt == 4))
            mm.then_inc(so_mm, 1)

            pe.wait_ge(fin_set, 1)
            for b in range(2):
                for n in range(2):
                    pe.wait_ge(g1_rep, 8 * b + 4 * n + 4)
                    for k in range(4):
                        mm = pe.transpose(ps[:, 4 + 2 * b + n, k * P:(k + 1) * P], D_REP[:, b, 4 * n + k, :], ident[:, :])
                    mm.then_inc(g1_mm, 1)
            pe.wait_ge(so_split, 1)
            pe.wait_ge(o_split, 8 * NPAIR)
            pe.wait_ge(wo_lo, KD)
            pe.wait_ge(wo_hi, KD)
            pe.wait_ge(g1_set, 4)

            def mix_out(t, s, first=False, rows=P):
                if not first:
                    pe.wait_ge(d_mo, t - 1)
                for n in range(2):
                    for k in range(KD):
                        for xh, wh in TERMS:
                            mm = pe.matmul(ps[0:rows, 2 * s + n, :], hidden_t[:, t, k, xh, 0:rows],
                                           D_WO[:, wh, k, 512 * n:512 * (n + 1)],
                                           start=(k == 0 and (xh, wh) == (0, 0)),
                                           stop=(k == KD - 1 and (xh, wh) == TERMS[-1]))
                mm.then_inc(d_mm, 1)

            mix_out(0, 0, True)
            mix_out(1, 1, True)
            mix_out(2, 0)
            turn(0, 0, D_XH, d_xhat, d_tr, 4, d_full, True)
            mix_out(3, 1)
            turn(1, 1, D_XH, d_xhat, d_tr, 4, d_full, True)
            with pe.Fori(2, 8) as i:
                for s in range(2):
                    mix_out(2 * i + s, s)
                    turn(2 * i + s - 2, s, D_XH, d_xhat, d_tr, 4, d_full)
            mix_out(16, 0, False, TS)
            turn(14, 0, D_XH, d_xhat, d_tr, 4, d_full)


            def gate_up(n, m, s, nb, grp, first=False):
                pe.wait_ge(gu_hi, n + 1)
                pe.wait_ge(gu_lo, n + 1)
                for blk in range(nb):
                    if not first:
                        pe.wait_ge(hid_set, m + blk + 1 - nb)
                    for w in range(2):
                        if blk < 2:
                            out = bank(2 * blk + w, BLK, 0)
                        else:
                            out = ps[:, 4, w * TS:(w + 1) * TS]
                        for k in range(KD):
                            for wh, xh in TERMS:
                                mm = pe.matmul(out, E_GHL[s][:, wh, k, w, :], moving(k, xh, 2 * grp + blk),
                                               start=(k == 0 and (wh, xh) == (0, 0)),
                                               stop=(k == KD - 1 and (wh, xh) == TERMS[-1]))
                    mm.then_inc(gu_mm, 1)

            def down(p, c, s):
                grp, blks, banks, m0 = PASSES[p]
                nb, m1 = len(blks), 2 * NF + 3 * NF * grp
                first = isinstance(c, int) and c == 0
                pe.wait_ge(wd_hi, 16 * p + 2 * c + 2)
                pe.wait_ge(wd_lo, 16 * p + 2 * c + 2)
                for i, blk in enumerate(blks):
                    if nb > 1 and not first:
                        pe.wait_ge(dn_out, m0 + nb * c + i + 1 - nb)
                    elif nb == 1 and c >= 2:
                        pe.wait_ge(dn_out, m0 + c - 1)
                    w = BLK if blk < 2 else TS
                    for j in range(NF):
                        if first and i == 0 and j == NF - 1:
                            pe.wait_ge(hid_hi, m1)
                            pe.wait_ge(hid_lo, m1)
                        for wh, xh in TERMS:
                            mm = pe.matmul(ps[:, banks[i if nb > 1 else s], 0:w], E_DHL[s][:, wh, j, :],
                                           E_HID[:, j, xh, BLK * blk:BLK * blk + w],
                                           start=(j == 0 and (wh, xh) == (0, 0)),
                                           stop=(j == NF - 1 and (wh, xh) == TERMS[-1]))
                    mm.then_inc(dn_mm, 1)

            def turn_back(n, s=0, wait=True):
                tile = LN2_TILES[n]
                rows = TS if tile == NT else P
                if wait:
                    pe.wait_ge(e_res, n if n <= 8 else n - 1)
                src = hidden_t[:, tile, :, :, :].bitcast(f32).rearrange("p k a t -> p (k a t)")
                for k in range(KD):
                    mm = pe.transpose(ps[0:rows, 5 - 2 * s + k // 4, (k % 4) * P:(k % 4 + 1) * P],
                                      src[:, k * P:k * P + rows], ident[:, :])
                mm.then_inc(e_tr, 1)

            for grp in range(2):
                nb = 2 + grp
                m0, n0 = 2 * NF * grp, NF * grp
                m1 = m0 + nb * NF
                if grp == 0:
                    pe.wait_ge(d_hi, 8)
                    pe.wait_ge(d_lo, 8)
                    pe.wait_ge(d_mo, NT + 1)
                else:
                    pe.wait_ge(dn_out, 16)
                for j in range(2):
                    gate_up(n0 + j, m0 + nb * j, j, nb, grp, j == 0)
                    if grp == 0 and j == 0:
                        turn(15, 1, D_XH, d_xhat, d_tr, 4, d_full)
                        turn(16, 0, D_XH, d_xhat, d_tr, 4, d_full, False, TS)
                        pe.wait_ge(d_hi, NT + 1)
                        pe.wait_ge(d_lo, NT + 1)
                    if grp == 1:
                        turn_back(j, 0, j > 0)
                if grp == 0:
                    with pe.Fori(1, NF // 2) as i:
                        for s in range(2):
                            gate_up(n0 + 2 * i + s, m0 + nb * (2 * i + s), s, nb, grp)
                else:
                    for j in range(2, 8):
                        gate_up(n0 + j, m0 + nb * j, j % 2, nb, grp)
                        turn_back(j)
                    with pe.Fori(4, NF // 2) as i:
                        for s in range(2):
                            gate_up(n0 + 2 * i + s, m0 + nb * (2 * i + s), s, nb, grp)
                pe.wait_ge(hid_hi, m1 - nb)
                pe.wait_ge(hid_lo, m1 - nb)
                pe.wait_ge(hid_set, m1)
                for c in range(2):
                    down(grp, c, c)
                with pe.Fori(1, KD // 2) as i:
                    for s in range(2):
                        down(grp, 2 * i + s, s)
            pe.wait_ge(dn_out, 32)
            for c in range(KD):
                if c < 5:
                    turn_back(8 + c, c % 2, c != 1)
                down(2, c, c % 2)
            pe.wait_ge(dn_out, 40)
            for n in range(13, NT + 1):
                turn_back(n, n % 2)
    return nc


INPUTS = ["x_prompt", "x_sample", "cache_k", "cache_v", "state_pool", "c_prompt", "c_sample",
          "w_ada", "b_ada", "w_in", "w_pool", "pool_scale", "w_o", "ln1_g", "ln1_b",
          "w_gu", "w_down", "ln2_g", "ln2_b"]
OUTPUTS = [(1, SEQ, D), (1, TS, D), (1, 1, SEQ, NH, HD), (1, 1, SEQ, NH, HD), (1, 1, HIST, PW),
           (1, 1, TS, NH, HD), (1, 1, TS, NH, HD), (1, 1, HIST, PW)]


def kernel(**inputs):
    import numpy as np
    import concourse.bacc as bacc
    from concourse.bass_utils import run_bass_kernel_spmd

    nc = bacc.Bacc("TRN2", target_bir_lowering=False, num_devices=1)
    arrays, args = {}, []
    for name in INPUTS:
        a = np.ascontiguousarray(inputs[name])
        arrays[f"in_{name}"] = a
        args.append(nc.dram_tensor(f"in_{name}", a.shape, mybir.dt.from_np(a.dtype), kind="ExternalInput").ap())
    for i, shape in enumerate(OUTPUTS):
        args.append(nc.dram_tensor(f"out_{i}", shape, f32, kind="ExternalOutput").ap())
    encoder_step(nc, *args)
    r = run_bass_kernel_spmd(nc, [arrays], core_ids=[0])
    return tuple(r.results[0][f"out_{i}"] for i in range(len(OUTPUTS)))
```
